# Optimizing a Trainium2 kernel written in Bass

```python
import jax, jax.numpy as jnp
from jax import lax
import numpy as np

D_MODEL = 1024
BATCH = 1
SEQ = 256
DEPTH = 2

N_EVEN = (DEPTH + 1) // 2
N_ODD = DEPTH // 2
EPS = 1e-6
ROPE_THETA = 500000.0
Q_BLOCK = 128

MOBA_HEADS = 8
MOBA_HEAD_DIM = 64
MOBA_ROT = MOBA_HEAD_DIM // 4
MOBA_BLOCK = 256
MOBA_TOPK = 3
RET_HEADS = 8
RET_DK = 64
RET_DV = 128
RET_CHUNK = 128
RET_THETA = 10000.0
MOBA_W = MOBA_HEADS * MOBA_HEAD_DIM
RET_QK_W = RET_HEADS * RET_DK
RET_V_W = RET_HEADS * RET_DV
EVEN_IN = 3 * MOBA_W + 2 * RET_QK_W + 2 * RET_V_W
EVEN_OUT = MOBA_W + RET_V_W
MLA_HEADS = 16
MLA_NOPE = 64
MLA_ROPE = 32
MLA_V = 64
MLA_Q_RANK = 512
MLA_KV_RANK = 256
MLA_DOWN = MLA_Q_RANK + MLA_KV_RANK + MLA_ROPE
PEER_HEADS = 8
PEER_NKEYS = 128
PEER_EXPERTS = PEER_NKEYS * PEER_NKEYS
PEER_DKEY = 128
PEER_TOPK = 16
PEER_CHUNK = 128

kernel_name = "hybrid_moba_retnet_mla_peer"

def rmsnorm(x, g):
    xf = x.astype(jnp.float32)
    y = xf * lax.rsqrt(jnp.mean(xf * xf, axis=-1, keepdims=True) + EPS)
    return (y * g).astype(x.dtype)

def rope_angles(S, rot_dim, theta):
    inv = 1.0 / (theta ** (jnp.arange(0, rot_dim, 2, dtype=jnp.float32) / rot_dim))
    ang = jnp.arange(S, dtype=jnp.float32)[:, None] * inv[None, :]
    return jnp.cos(ang), jnp.sin(ang)

def apply_rope(x, cos, sin):
    r2 = x.shape[-1] // 2
    x1, x2 = x[..., :r2], x[..., r2:]
    c = cos[None, :, None, :]
    s = sin[None, :, None, :]
    return jnp.concatenate([x1 * c - x2 * s, x2 * c + x1 * s], axis=-1).astype(x.dtype)

def partial_rope(x, cos, sin, rot):
    return jnp.concatenate([apply_rope(x[..., :rot], cos, sin), x[..., rot:]], axis=-1)

def moba_attention(q, k, v):
    B, S, H, D = q.shape
    pad = (-S) % MOBA_BLOCK
    padw = ((0, 0), (0, pad), (0, 0), (0, 0))
    q, k, v = jnp.pad(q, padw), jnp.pad(k, padw), jnp.pad(v, padw)
    Sp = S + pad
    nb = Sp // MOBA_BLOCK
    nq = Sp // Q_BLOCK
    kb = k.reshape(B, nb, MOBA_BLOCK, H, D).transpose(0, 3, 1, 2, 4)
    vb = v.reshape(B, nb, MOBA_BLOCK, H, D).transpose(0, 3, 1, 2, 4)
    kmean = jnp.mean(kb.astype(jnp.float32), axis=3)
    n_sel = min(MOBA_TOPK, nb - 1)
    scale = D ** -0.5
    bi = jnp.arange(B)[:, None, None, None]
    hi = jnp.arange(H)[None, :, None, None]

    def one_block(c):
        q0 = c * Q_BLOCK
        qs = lax.dynamic_slice_in_dim(q, q0, Q_BLOCK, axis=1)
        blk = q0 // MOBA_BLOCK
        qpos = q0 + jnp.arange(Q_BLOCK)
        kpos = blk * MOBA_BLOCK + jnp.arange(MOBA_BLOCK)
        kown = lax.dynamic_index_in_dim(kb, blk, axis=2, keepdims=False)
        vown = lax.dynamic_index_in_dim(vb, blk, axis=2, keepdims=False)
        s_own = jnp.einsum("bqhd,bhkd->bhqk", qs, kown).astype(jnp.float32) * scale
        s_own = jnp.where(kpos[None, :] <= qpos[:, None], s_own, -jnp.inf)
        if n_sel == 0:
            p = jax.nn.softmax(s_own, axis=-1)
            return jnp.einsum("bhqk,bhkd->bqhd", p, vown)
        gate = jnp.einsum("bqhd,bhnd->bhqn", qs.astype(jnp.float32), kmean)
        gate = jnp.where(jnp.arange(nb) < blk, gate, -jnp.inf)
        _, idx = lax.top_k(gate, n_sel)
        ksel = kb[bi, hi, idx]
        vsel = vb[bi, hi, idx]
        s_sel = jnp.einsum("bqhd,bhqnkd->bhqnk", qs, ksel).astype(jnp.float32) * scale
        valid = jnp.arange(n_sel) < blk
        s_sel = jnp.where(valid[:, None], s_sel, -jnp.inf).reshape(B, H, Q_BLOCK, n_sel * MOBA_BLOCK)
        p = jax.nn.softmax(jnp.concatenate([s_sel, s_own], axis=-1), axis=-1)
        p_sel = p[..., : n_sel * MOBA_BLOCK].reshape(B, H, Q_BLOCK, n_sel, MOBA_BLOCK)
        p_own = p[..., n_sel * MOBA_BLOCK:]
        return (jnp.einsum("bhqnk,bhqnkd->bqhd", p_sel, vsel)
                + jnp.einsum("bhqk,bhkd->bqhd", p_own, vown))

    o = lax.map(one_block, jnp.arange(nq))
    return o.transpose(1, 0, 2, 3, 4).reshape(B, Sp, H, D)[:, :S]

def retention_chunkwise(q, k, v):
    B, S, H, dk = q.shape
    dv = v.shape[-1]
    C = RET_CHUNK
    n = S // C
    log_g = jnp.log(1.0 - 2.0 ** (-5.0 - jnp.arange(H, dtype=jnp.float32)))
    pos = jnp.arange(C, dtype=jnp.float32)
    diff = pos[:, None] - pos[None, :]
    dmat = jnp.where(diff >= 0, jnp.exp(log_g[:, None, None] * jnp.maximum(diff, 0.0)), 0.0)
    xi = jnp.exp(log_g[:, None] * (pos + 1.0))[None, :, :, None]
    zeta = jnp.exp(log_g[:, None] * (C - 1.0 - pos))[None, :, :, None]
    g_chunk = jnp.exp(log_g * C)[None, :, None, None]

    def to_chunks(t):
        return t.astype(jnp.float32).reshape(B, n, C, H, t.shape[-1]).transpose(1, 0, 3, 2, 4)

    def body(R, xs):
        qi, ki, vi = xs
        inner = jnp.einsum("bhnd,bhmd->bhnm", qi, ki) * dmat[None]
        out = jnp.einsum("bhnm,bhme->bhne", inner, vi) + jnp.einsum("bhnd,bhde->bhne", qi, R) * xi
        R_new = R * g_chunk + jnp.einsum("bhmd,bhme->bhde", ki * zeta, vi)
        return R_new, out

    R0 = jnp.zeros((B, H, dk, dv), jnp.float32)
    _, o = lax.scan(body, R0, (to_chunks(q), to_chunks(k), to_chunks(v)))
    return o.transpose(1, 0, 3, 2, 4).reshape(B, S, H, dv)

def causal_attention_blocked(q, k, v):
    B, S, H, dq = q.shape
    nq = S // Q_BLOCK
    scale = dq ** -0.5
    kpos = jnp.arange(S)

    def one_block(c):
        q0 = c * Q_BLOCK
        qs = lax.dynamic_slice_in_dim(q, q0, Q_BLOCK, axis=1)
        s = jnp.einsum("bqhd,bkhd->bhqk", qs, k).astype(jnp.float32) * scale
        qpos = q0 + jnp.arange(Q_BLOCK)
        s = jnp.where(kpos[None, :] <= qpos[:, None], s, -jnp.inf)
        p = jax.nn.softmax(s, axis=-1)
        return jnp.einsum("bhqk,bkhd->bqhd", p, v)

    o = lax.map(one_block, jnp.arange(nq))
    return o.transpose(1, 0, 2, 3, 4).reshape(B, S, H, v.shape[-1])

def even_mixer(h, w_in, ret_gn, w_o):
    B, S, _ = h.shape
    proj = h @ w_in
    splits = [MOBA_W, 2 * MOBA_W, 3 * MOBA_W, 3 * MOBA_W + RET_QK_W,
              3 * MOBA_W + 2 * RET_QK_W, 3 * MOBA_W + 2 * RET_QK_W + RET_V_W]
    mq, mk, mv, rq, rk, rv, rg = jnp.split(proj, splits, axis=-1)
    cos_m, sin_m = rope_angles(S, MOBA_ROT, ROPE_THETA)
    mq = partial_rope(mq.reshape(B, S, MOBA_HEADS, MOBA_HEAD_DIM), cos_m, sin_m, MOBA_ROT)
    mk = partial_rope(mk.reshape(B, S, MOBA_HEADS, MOBA_HEAD_DIM), cos_m, sin_m, MOBA_ROT)
    mv = mv.reshape(B, S, MOBA_HEADS, MOBA_HEAD_DIM)
    a_out = moba_attention(mq, mk, mv).reshape(B, S, MOBA_W)
    cos_r, sin_r = rope_angles(S, RET_DK, RET_THETA)
    rq = apply_rope(rq.reshape(B, S, RET_HEADS, RET_DK), cos_r, sin_r)
    rk = apply_rope(rk.reshape(B, S, RET_HEADS, RET_DK), cos_r, sin_r) * (RET_DK ** -0.5)
    rv = rv.reshape(B, S, RET_HEADS, RET_DV)
    r = retention_chunkwise(rq, rk, rv)
    mu = jnp.mean(r, axis=-1, keepdims=True)
    var = jnp.mean(jnp.square(r - mu), axis=-1, keepdims=True)
    r = ((r - mu) * lax.rsqrt(var + EPS)) * ret_gn.reshape(RET_HEADS, RET_DV)
    b_out = r.reshape(B, S, RET_V_W) * jax.nn.silu(rg.astype(jnp.float32))
    cat = jnp.concatenate([a_out.astype(jnp.float32), b_out], axis=-1).astype(h.dtype)
    return cat @ w_o

def odd_mixer(h, w_down, q_norm, w_uq, kv_norm, w_ukv, w_o):
    B, S, _ = h.shape
    down = h @ w_down
    cq, ckv, kr = jnp.split(down, [MLA_Q_RANK, MLA_Q_RANK + MLA_KV_RANK], axis=-1)
    cq = rmsnorm(cq, q_norm)
    ckv = rmsnorm(ckv, kv_norm)
    q = (cq @ w_uq).reshape(B, S, MLA_HEADS, MLA_NOPE + MLA_ROPE)
    cos, sin = rope_angles(S, MLA_ROPE, ROPE_THETA)
    q_rope = apply_rope(q[..., MLA_NOPE:], cos, sin)
    k_rope = apply_rope(kr[:, :, None, :], cos, sin)
    kv = (ckv @ w_ukv).reshape(B, S, MLA_HEADS, MLA_NOPE + MLA_V)
    k_nope, v = kv[..., :MLA_NOPE], kv[..., MLA_NOPE:]
    qf = jnp.concatenate([q[..., :MLA_NOPE], q_rope], axis=-1)
    kf = jnp.concatenate([k_nope, jnp.broadcast_to(k_rope, (B, S, MLA_HEADS, MLA_ROPE)).astype(k_nope.dtype)], axis=-1)
    o = causal_attention_blocked(qf, kf, v)
    return o.reshape(B, S, MLA_HEADS * MLA_V).astype(h.dtype) @ w_o

def peer_ffn(x, w_q, sub_keys, u_tab, v_tab):
    B, S, D = x.shape
    T = B * S
    KK = PEER_TOPK * PEER_TOPK
    xt = x.reshape(T, D)
    qry = (xt @ w_q).reshape(T, PEER_HEADS, 2, PEER_DKEY // 2).astype(jnp.float32)
    s = jnp.einsum("thpd,hpnd->thpn", qry, sub_keys.astype(jnp.float32))
    s1, i1 = lax.top_k(s[:, :, 0], PEER_TOPK)
    s2, i2 = lax.top_k(s[:, :, 1], PEER_TOPK)
    cand = (s1[..., :, None] + s2[..., None, :]).reshape(T, PEER_HEADS, KK)
    cidx = (i1[..., :, None] * PEER_NKEYS + i2[..., None, :]).reshape(T, PEER_HEADS, KK)
    top_s, pos = lax.top_k(cand, PEER_TOPK)
    eidx = jnp.take_along_axis(cidx, pos, axis=-1)
    gate = jax.nn.softmax(top_s, axis=-1)
    nc = T // PEER_CHUNK

    def chunk(args):
        xc, ec, gc = args
        ue = u_tab[ec]
        ve = v_tab[ec]
        a = jax.nn.gelu(jnp.einsum("td,thkd->thk", xc, ue), approximate=False) * gc
        return jnp.einsum("thk,thkd->td", a, ve)

    out = lax.map(chunk, (xt.reshape(nc, PEER_CHUNK, D),
                          eidx.reshape(nc, PEER_CHUNK, PEER_HEADS, PEER_TOPK),
                          gate.reshape(nc, PEER_CHUNK, PEER_HEADS, PEER_TOPK)))
    return out.reshape(B, S, D).astype(x.dtype)

def setup_inputs(seed: int = 0) -> dict:
    key = jax.random.key(seed)
    ks = jax.random.split(key, 17)
    f32 = jnp.float32

    def nrm(k, shape, scale):
        return jax.random.normal(k, shape, f32) * scale

    def gain(k, shape):
        return 1.0 + 0.02 * jax.random.normal(k, shape, f32)

    return {
        "x": nrm(ks[0], (BATCH, SEQ, D_MODEL), 1.0),
        "attn_norm": gain(ks[1], (DEPTH, D_MODEL)),
        "ffn_norm": gain(ks[2], (DEPTH, D_MODEL)),
        "ev_w_in": nrm(ks[3], (N_EVEN, D_MODEL, EVEN_IN), D_MODEL ** -0.5),
        "ev_ret_gn": gain(ks[4], (N_EVEN, RET_V_W)),
        "ev_w_o": nrm(ks[5], (N_EVEN, EVEN_OUT, D_MODEL), EVEN_OUT ** -0.5),
        "od_w_down": nrm(ks[6], (N_ODD, D_MODEL, MLA_DOWN), D_MODEL ** -0.5),
        "od_q_norm": gain(ks[7], (N_ODD, MLA_Q_RANK)),
        "od_w_uq": nrm(ks[8], (N_ODD, MLA_Q_RANK, MLA_HEADS * (MLA_NOPE + MLA_ROPE)), MLA_Q_RANK ** -0.5),
        "od_kv_norm": gain(ks[9], (N_ODD, MLA_KV_RANK)),
        "od_w_ukv": nrm(ks[10], (N_ODD, MLA_KV_RANK, MLA_HEADS * (MLA_NOPE + MLA_V)), MLA_KV_RANK ** -0.5),
        "od_w_o": nrm(ks[11], (N_ODD, MLA_HEADS * MLA_V, D_MODEL), (MLA_HEADS * MLA_V) ** -0.5),
        "peer_wq": nrm(ks[12], (DEPTH, D_MODEL, PEER_HEADS * PEER_DKEY), D_MODEL ** -0.5),
        "peer_keys": nrm(ks[13], (DEPTH, PEER_HEADS, 2, PEER_NKEYS, PEER_DKEY // 2), (PEER_DKEY // 2) ** -0.5),
        "peer_u": nrm(ks[14], (DEPTH, PEER_EXPERTS, D_MODEL), D_MODEL ** -0.5),
        "peer_v": nrm(ks[15], (DEPTH, PEER_EXPERTS, D_MODEL), PEER_HEADS ** -0.5),
        "final_norm": gain(ks[16], (D_MODEL,)),
    }

def reference(x, attn_norm, ffn_norm, ev_w_in, ev_ret_gn, ev_w_o, od_w_down, od_q_norm, od_w_uq,
              od_kv_norm, od_w_ukv, od_w_o, peer_wq, peer_keys, peer_u, peer_v, final_norm):
    h = x
    for i in range(DEPTH):
        hn = rmsnorm(h, attn_norm[i])
        j = i // 2
        if i % 2 == 0:
            mix = even_mixer(hn, ev_w_in[j], ev_ret_gn[j], ev_w_o[j])
        else:
            mix = odd_mixer(hn, od_w_down[j], od_q_norm[j], od_w_uq[j], od_kv_norm[j], od_w_ukv[j], od_w_o[j])
        h = h + mix.astype(h.dtype)
        h = h + peer_ffn(rmsnorm(h, ffn_norm[i]), peer_wq[i], peer_keys[i], peer_u[i], peer_v[i])
    return rmsnorm(h, final_norm).astype(x.dtype)


_drawn_inputs = setup_inputs


def setup_inputs(seed=0):
    import zlib

    import numpy as np

    out = dict(_drawn_inputs(seed))
    spreads = {}
    factors = {'od_q_norm': 6.715, 'od_kv_norm': 4.529, 'final_norm': 2.86}
    for name, (base, spread) in spreads.items():
        noise = np.random.default_rng([zlib.crc32(name.encode()), seed]).standard_normal(out[name].shape)
        drawn = base * np.exp(spread * noise) if base else spread * noise
        out[name] = __import__('jax').numpy.asarray(drawn.astype(out[name].dtype))
    for name, factor in factors.items():
        out[name] = (out[name] * factor).astype(out[name].dtype)
    return out
```

```python
from contextlib import ExitStack

import numpy as np

import concourse.bass as bass
from concourse import mybir

ALU = mybir.AluOpType
ACT = mybir.ActivationFunctionType
AX_X = mybir.AxisListType.X
F32 = mybir.dt.float32
F32R = mybir.dt.float32r
U32 = mybir.dt.uint32

P = 128
SEQ = 256
TT = SEQ // P
D = 1024
KC = D // P
EPS = 1e-6
ROPE_THETA, RET_THETA = 500000.0, 10000.0

MOBA_H, MOBA_D, MOBA_ROT = 8, 64, 16
RET_H, RET_DK, RET_DV = 8, 64, 128
MOBA_W, RET_QK_W, RET_V_W = MOBA_H * MOBA_D, RET_H * RET_DK, RET_H * RET_DV
COL_MV = 2 * MOBA_W
COL_RQ = 3 * MOBA_W
COL_RV = COL_RQ + 2 * RET_QK_W
COL_RG = COL_RV + RET_V_W
EVEN_IN = COL_RG + RET_V_W
EVEN_OUT = MOBA_W + RET_V_W
MLA_H, MLA_NOPE, MLA_ROPE, MLA_V = 16, 64, 32, 64
MLA_QD = MLA_NOPE + MLA_ROPE
Q_RANK, KV_RANK = 512, 256
MLA_DOWN = Q_RANK + KV_RANK + MLA_ROPE
PEER_H, NKEYS, TOPK = 8, 128, 16
NEXP = NKEYS * NKEYS
PICKS = PEER_H * TOPK
LISTS = TT * PEER_H * 2
HEADS = TT * PEER_H

UW = 1024
HB = 512
RING = 4
SPLITS = 2
FLIGHT = 4
LOWEST = -3.0e38

C_ID = 0
C_IOTA = C_ID + P
C_MASK = C_IOTA + P
C_MROPE = C_MASK + 3 * P
C_RROPE = C_MROPE + 2 * TT * (MOBA_ROT // 2)
C_LROPE = C_RROPE + 2 * TT * (RET_DK // 2)
C_EPS = C_LROPE + 2 * TT * (MLA_ROPE // 2)
C_END = C_EPS + 1

G_ATTN0, G_FFN0, G_ATTN1, G_FFN1 = 0, KC, 2 * KC, 3 * KC
G_Q = 4 * KC
G_KV = G_Q + Q_RANK // P
G_END = G_KV + KV_RANK // P


def rope_table(rot, theta):
    inv = (1.0 / (np.float32(theta) ** (np.arange(0, rot, 2, dtype=np.float32) / np.float32(rot)))).astype(np.float32)
    ang = np.arange(SEQ, dtype=np.float32)[:, None] * inv[None, :]
    cs = np.stack([np.cos(ang), np.sin(ang)]).astype(np.float32)
    return cs.reshape(2, TT, P, rot // 2).transpose(2, 0, 1, 3).reshape(P, -1)


def constants():
    tri = np.where(np.arange(P)[None, :] <= np.arange(P)[:, None], 0.0, -1.0e30)
    c = np.concatenate([np.eye(P), np.tile(np.arange(P), (P, 1)), tri, np.zeros((P, P)), tri,
                        rope_table(MOBA_ROT, ROPE_THETA), rope_table(RET_DK, RET_THETA),
                        rope_table(MLA_ROPE, ROPE_THETA), np.full((P, 1), EPS)], axis=1)
    assert c.shape[1] == C_END
    return c.astype(np.float32)


def decay_table():
    log_g = np.log(1.0 - 2.0 ** (-5.0 - np.arange(RET_H)))
    diff = np.arange(SEQ)[None, :] - np.arange(P)[:, None]
    d = np.where(diff[:, None, :] >= 0, np.exp(log_g[None, :, None] * np.maximum(diff, 0)[:, None, :]), 0.0)
    return (d * RET_DK ** -0.5).astype(np.float32)


IN_FULL = EVEN_IN // UW
SEG = {}
_at = 0
for _name, _n in (("in", IN_FULL * KC + KC // 2), ("eo", EVEN_OUT // P), ("q0", PEER_H), ("u0", NKEYS), ("v0", NKEYS),
                  ("down", KC), ("uq", 6), ("ukv", 4), ("oo", KC), ("q1", PEER_H), ("u1", NKEYS), ("v1", NKEYS)):
    SEG[_name] = (_at, _n)
    _at += _n
N_UNITS = _at

TURNS = (("attn0", 0, KC, G_ATTN0), ("cat", 0, EVEN_OUT // P, None), ("ffn0", 0, KC, G_FFN0),
         ("attn1", 0, KC, G_ATTN1), ("down", 0, (Q_RANK + KV_RANK) // P, G_Q), ("heads", 0, KC, None),
         ("ffn1", 0, KC, G_FFN1))
TURN_AT = {}
_at = 0
for _name, _c0, _n, _g in TURNS:
    TURN_AT[_name] = (_at, _c0, _n, _g)
    _at += _n
TURN_NO = {t[0]: i for i, t in enumerate(TURNS)}


def blocks_of(seg):
    u0, _ = SEG[seg]
    if seg == "in":
        first = u0 + IN_FULL * KC
        return [([(first + n, [(2 * n, 0), (2 * n + 1, HB)]) for n in range(KC // 2)], [HB])]
    if seg == "eo":
        return [([(u0 + c, [(c, 0)]) for c in range(EVEN_OUT // P)], [HB, HB])]
    if seg == "down":
        return [([(u0 + c, [(c, 0)]) for c in range(KC)], [MLA_DOWN // 2, MLA_DOWN // 2])]
    if seg == "uq":
        return [([(u0 + c, [(c, 0)]) for c in range(4)], [HB, HB]),
                ([(u0 + 4 + n, [(2 * n, 0), (2 * n + 1, HB)]) for n in range(2)], [HB])]
    if seg == "ukv":
        return [([(u0 + 2 * b + n, [(4 + n, 0)]) for n in range(2)], [HB, HB]) for b in range(2)]
    return [([(u0 + c, [(c, 0)]) for c in range(KC)], [HB, HB])]


def build(nc, x, w, peer_keys, gains, gn_gain, fin_gain, consts, decay, out):
    with ExitStack() as ctx:
        def sb(name, shape, dt=F32, scope=ctx):
            return scope.enter_context(nc.sbuf_tensor(name, shape, dt))

        def sem(name):
            return ctx.enter_context(nc.semaphore(name))

        cst = sb("cst", [P, C_END])
        gain = sb("gain", [P, G_END])
        h = sb("h", [P, TT, D])
        xt_hi = sb("xt_hi", [P, KC, SEQ], F32R)
        xt_lo = sb("xt_lo", [P, KC, SEQ], F32R)
        xt_f = sb("xt_f", [P, FLIGHT, SEQ])
        raw = sb("raw", [P, RING, UW])
        w_hi = sb("w_hi", [P, SPLITS, UW], F32R)
        w_lo = sb("w_lo", [P, SPLITS, UW], F32R)
        stat = sb("stat", [P, 8])
        picks = sb("picks", [P, 3, HEADS, TOPK])
        gsum = sb("gsum", [P, 2, HEADS])

        s0 = ExitStack()
        xn0 = sb("xn0", [P, TT, D], F32, s0)
        xt2_hi = sb("xt2_hi", [P, 4, SEQ], F32R, s0)
        xt2_lo = sb("xt2_lo", [P, 4, SEQ], F32R, s0)
        proj = sb("proj", [P, TT, EVEN_IN], F32, s0)
        qk_t = sb("qk_t", [P, 16, SEQ], F32, s0)
        dec = sb("dec", [P, RET_H, SEQ], F32, s0)
        cat = sb("cat", [P, TT, EVEN_OUT], F32, s0)
        sc0 = sb("sc0", [P, 2, 3 * P], F32, s0)
        pr0 = sb("pr0", [P, 2, 3 * P], F32, s0)
        pt0 = sb("pt0", [P, 2, 3 * P], F32, s0)
        row0 = sb("row0", [P, 6, TT, MOBA_H], F32, s0)
        tmp0 = sb("tmp0", [P, 4, TT * 16 * 32], F32, s0)
        gnb = sb("gnb", [P, RET_V_W], F32, s0)
        gns = sb("gns", [P, 4, TT, RET_H], F32, s0)
        s0.close()
        s1 = ExitStack()
        xn1 = sb("xn1", [P, TT, D], F32, s1)
        down = sb("down", [P, TT, MLA_DOWN], F32, s1)
        q1 = sb("q1", [P, TT, MLA_H * MLA_QD], F32, s1)
        kv = sb("kv", [P, TT, MLA_H * (MLA_NOPE + MLA_V)], F32, s1)
        kf = sb("kf", [P, TT, MLA_H * MLA_QD], F32, s1)
        q_t = sb("q_t", [MLA_QD, MLA_H, SEQ], F32, s1)
        k_t = sb("k_t", [MLA_QD, MLA_H, SEQ], F32, s1)
        sc1 = sb("sc1", [P, 2, 3 * P], F32, s1)
        pr1 = sb("pr1", [P, 2, 3 * P], F32, s1)
        pt1 = sb("pt1", [P, 2, 3 * P], F32, s1)
        row1 = sb("row1", [P, 6, TT, MLA_H], F32, s1)
        tmp1 = sb("tmp1", [P, 4, TT * MLA_H * 16], F32, s1)
        o1 = sb("o1", [P, TT, D], F32, s1)
        s1.close()
        s2 = ExitStack()
        a_t = sb("a_t", [P, NKEYS, SEQ], F32, s2)
        s3 = ExitStack()
        best = sb("best", [P, LISTS, TOPK], F32, s3)
        best_i = sb("best_i", [P, LISTS, TOPK], F32, s3)
        tops = sb("tops", [P, HEADS, TOPK], F32, s3)
        lst = sb("lst", [P, NKEYS], F32, s3)
        v16 = sb("v16", [P, TOPK], F32, s3)
        n16 = sb("n16", [P, 3, TOPK], U32, s3)
        f16 = sb("f16", [P, 2, TOPK], F32, s3)
        cand = sb("cand", [P, TOPK, TOPK], F32, s3)
        eqs = sb("eqs", [P, 2, TOPK, TOPK], F32, s3)
        s3.close()
        s4 = ExitStack()
        pick_t = sb("pick_t", [P, 3, SEQ], F32, s4)
        hot2 = sb("hot2", [P, 8, P], F32, s4)
        hot1 = sb("hot1", [P, 8, P], F32, s4)
        s4.close()
        s5 = ExitStack()
        ga_hi = sb("ga_hi", [P, 2, SEQ], F32R, s5)
        ga_lo = sb("ga_lo", [P, 2, SEQ], F32R, s5)
        s5.close()
        s2.close()
        s6 = ExitStack()
        fin = sb("fin", [P, TT, D], F32, s6)
        fing = sb("fing", [P, D], F32, s6)
        kys = sb("kys", [P, PEER_H, NKEYS], F32, s6)
        qry_t = sb("qry_t", [P, PEER_H, SEQ], F32, s6)
        s6.close()
        S_TILES = LISTS * NKEYS // SEQ
        scores = a_t[:, NKEYS - S_TILES:, :].rearrange("p a (b n) -> p (a b) n", n=NKEYS)

        acc = [ctx.enter_context(nc.psum_tensor(f"acc{i}", [P, HB], F32)) for i in range(4)]
        sco = [ctx.enter_context(nc.psum_tensor(f"sco{i}", [P, HB], F32)) for i in range(2)]
        trn = [ctx.enter_context(nc.psum_tensor(f"trn{i}", [P, HB], F32)) for i in range(2)]

        s_cst = sem("s_cst")
        s_dec = sem("s_dec")
        s_keys = sem("s_keys")
        s_fing = sem("s_fing")
        s_out = sem("s_out")
        raw_in = [sem(f"raw_in{i}") for i in range(RING)]
        hi_ready = sem("hi_ready")
        lo_ready = sem("lo_ready")
        unit_used = sem("unit_used")
        act_step = sem("act_step")
        dve_step = sem("dve_step")
        src_ready = sem("src_ready")
        turn_ps = sem("turn_ps")
        turn_f = sem("turn_f")
        turn_hi = sem("turn_hi")
        turn_lo = sem("turn_lo")
        sq_ready = sem("sq_ready")
        ms_ready = sem("ms_ready")
        blk_act = sem("blk_act")
        blk_dve = sem("blk_dve")
        roped = sem("roped")
        hd_ps = sem("hd_ps")
        hd_act = sem("hd_act")
        hd_dve = sem("hd_dve")
        qk_ps = sem("qk_ps")
        masked = sem("masked")
        probs = sem("probs")
        pt_ps = sem("pt_ps")
        pt_ready = sem("pt_ready")
        pv_done = sem("pv_done")
        o_read = sem("o_read")
        cen_ready = sem("cen_ready")
        var_ready = sem("var_ready")
        vsum_ready = sem("vsum_ready")
        swish = sem("swish")
        a_read = sem("a_read")
        s_ps = sem("s_ps")
        s_rd = sem("s_rd")
        listed = sem("listed")
        shifted = sem("shifted")
        expd = sem("expd")
        gated = sem("gated")
        pk_ps = sem("pk_ps")
        pk_rd = sem("pk_rd")
        hot_ready = sem("hot_ready")
        g_ps = sem("g_ps")
        g_rd = sem("g_rd")
        ga_hi_ready = sem("ga_hi_ready")
        ga_lo_ready = sem("ga_lo_ready")

        ident = cst[:, C_ID:C_ID + P]
        iota = cst[:, C_IOTA:C_IOTA + P]
        iota16 = cst[:, C_IOTA:C_IOTA + TOPK]
        eps = cst[:, C_EPS:C_EPS + 1]

        def table(at, n):
            t = cst[:, at:at + 2 * TT * n].rearrange("p (k t n) -> p k t n", k=2, t=TT)
            return t[:, 0], t[:, 1]

        def xt(c):
            return (xt_hi[:, c, :], xt_lo[:, c, :]) if c < KC else (xt2_hi[:, c - KC, :], xt2_lo[:, c - KC, :])

        def spread(ap, shape, axis):
            return ap.unsqueeze(axis).to_broadcast(shape)

        NH0 = 16
        HD0 = NH0
        QK_AT = {"moba": 0, "ret": MOBA_H, "mla": MOBA_H + RET_H}
        PR_AT = {"moba": 0, "mla": MOBA_H}

        block = ctx.enter_context(nc.Block())

        @block.sync
        def _(sp):
            def load(u, src, at=0):
                if u >= RING:
                    sp.wait_ge(lo_ready, u - RING + 1 + at)
                sp.dma_start(raw[:, u % RING, :], src).then_inc(raw_in[u % RING], 16)

            def segment(name, first=0):
                u0, n = SEG[name]
                u = u0 + first
                if first == 0 and u0 == 0:
                    for k in range(RING):
                        load(k, w[name][k])
                    u = RING
                whole = (u0 + n - u) // RING * RING
                if whole > RING:
                    with sp.Fori(0, whole // RING) as i:
                        for k in range(RING):
                            load(u + k, w[name][i * RING + (u - u0 + k)], i * RING)
                    u += whole
                while u < u0 + n:
                    load(u, w[name][u - u0])
                    u += 1

            sp.dma_start(h[:], x).then_inc(s_cst, 16)
            sp.dma_start(cst[:], consts).then_inc(s_cst, 16)
            sp.dma_start(gain[:], gains).then_inc(s_cst, 16)
            sp.dma_start(dec[:], decay).then_inc(s_dec, 16)
            sp.dma_start(gnb[:], gn_gain.partition_broadcast(P)).then_inc(s_dec, 16)
            segment("in")
            segment("eo")
            for layer in range(2):
                segment(f"q{layer}")
                sp.wait_ge(unit_used, SEG[f"q{layer}"][0])
                sp.dma_start(kys[:], peer_keys[layer]).then_inc(s_keys, 16)
                segment(f"u{layer}")
                segment(f"v{layer}")
                if layer == 0:
                    for name in ("down", "uq", "ukv", "oo"):
                        segment(name)
            sp.wait_ge(unit_used, N_UNITS)
            sp.dma_start(fing[:], fin_gain.partition_broadcast(P)).then_inc(s_fing, 16)
            sp.wait_ge(src_ready, len(TURNS) + 1)
            sp.dma_start(out, fin[:]).then_inc(s_out, 16)
            sp.wait_ge(s_out, 16)

        @block.scalar
        def _(act):
            nxt = [0]
            own = [0]

            def hi(u, at=0):
                act.wait_ge(raw_in[u % RING], 16 * (u // RING + 1) + at * (16 // RING))
                if u >= SPLITS or not isinstance(at, int):
                    act.wait_ge(unit_used, u - SPLITS + 1 + at)
                act.activation(w_hi[:, u % SPLITS, :], raw[:, u % RING, :], ACT.Copy).then_inc(hi_ready, 1)

            def hi_until(u):
                while nxt[0] < min(u, N_UNITS):
                    hi(nxt[0])
                    nxt[0] += 1

            def turn(name):
                at, c0, n, _ = TURN_AT[name]
                for c in range(n):
                    act.wait_ge(turn_f, at + c + 1)
                    act.activation(xt(c0 + c)[0], xt_f[:, (at + c) % FLIGHT, :], ACT.Copy).then_inc(turn_hi, 1)

            def squares(n_at, srcs, width):
                act.wait_ge(ms_ready, n_at + 1)
                for k, (src, scratch) in enumerate(srcs):
                    act.activation(scratch, src, ACT.Square, accum_out=stat[:, k:k + 1]).then_inc(act_step, 1)
                    own[0] += 1
                act.wait_ge(act_step, own[0])
                for k in range(len(srcs)):
                    ins = act.activation(stat[:, 4 + k:5 + k], stat[:, k:k + 1], ACT.Sqrt, bias=eps, scale=1.0 / width[k])
                    if k < len(srcs) - 1:
                        own[0] += 1
                        ins.then_inc(act_step, 1)
                    else:
                        ins.then_inc(sq_ready, 1)
                act.wait_ge(act_step, own[0])

            def block_out(n, dests):
                act.wait_ge(unit_used, n)
                for k, (dst, src) in enumerate(dests):
                    ins = act.activation(dst, src, ACT.Copy)
                ins.then_inc(blk_act, 1)

            def heads_out(at, n, dst):
                for k in range(0, n, 2):
                    act.wait_ge(hd_ps, at + k + 1)
                    act.activation(dst(k), trn[k % 2][0:dst(k).shape[0], 0:SEQ], ACT.Copy).then_inc(hd_act, 1)

            def softmax(name, heads, sc, pr, row, scale):
                at = PR_AT[name]
                for n in range(heads):
                    act.wait_ge(masked, QK_AT[name] + n + 1)
                    if at + n >= 2:
                        act.wait_ge(pt_ps, at + n - 1)
                    act.activation(pr[:, n % 2, 0:P], sc[:, n % 2, 0:P], ACT.Exp, bias=row[:, 1, 0, n:n + 1],
                                   scale=scale, accum_out=row[:, 2, 0, n:n + 1])
                    act.activation(pr[:, n % 2, P:3 * P], sc[:, n % 2, P:3 * P], ACT.Exp, bias=row[:, 1, 1, n:n + 1],
                                   scale=scale, accum_out=row[:, 2, 1, n:n + 1]).then_inc(probs, 1)

            def peer(layer):
                u0, n = SEG[f"q{layer}"]
                for k in range(n):
                    hi_until(u0 + k + 2)
                    act.wait_ge(unit_used, u0 + k + 1)
                    act.activation(qry_t[:, k, :], sco[k % 2][:, 0:SEQ], ACT.Copy).then_inc(a_read, 1)
                u0, n = SEG[f"u{layer}"]
                for half in range(2):
                    if half:
                        act.wait_ge(listed, layer + 1)
                    else:
                        act.wait_ge(s_rd, (layer + 1) * (LISTS // 4))
                    at = half * (n // 2)
                    with act.Fori(0, n // 2 // RING) as i:
                        for k in range(RING):
                            hi(u0 + at + k + 1, i * RING)
                            act.wait_ge(unit_used, i * RING + (u0 + at + k + 1))
                            act.activation(a_t[:, i * RING + (at + k), :], sco[k % 2][:, 0:SEQ],
                                           ACT.Gelu).then_inc(a_read, 1)
                nxt[0] += n
                act.wait_ge(shifted, layer + 1)
                act.activation(tops[:], tops[:], ACT.Exp).then_inc(expd, 1)
                u0, n = SEG[f"v{layer}"]
                act.wait_ge(g_rd, (layer + 1) * (SEQ // 4))
                with act.Fori(0, n // RING - 1) as i:
                    for k in range(RING):
                        gate_tile(layer, i * RING, k)
                        hi(u0 + k + 1, i * RING)
                nxt[0] += n - RING
                for k in range(n - RING, n):
                    gate_tile(layer, 0, k)
                    hi_until(u0 + k + 2)

            def gate_tile(layer, i, k):
                act.wait_ge(unit_used, i + (SEG[f"v{layer}"][0] + k - 1))
                act.activation(ga_hi[:, k % 2, :], a_t[:, i + k, :], ACT.Copy).then_inc(ga_hi_ready, 1)

            act.wait_ge(s_cst, 48)
            squares(0, [(h[:, t, :], xn0[:, t, :]) for t in range(TT)], [D] * TT)
            hi_until(1)
            turn("attn0")
            with act.Fori(0, IN_FULL) as i:
                for k in range(KC):
                    hi(k + 1, i * KC)
                act.wait_ge(unit_used, i * KC + KC)
                for half in range(2):
                    ins = act.activation(proj[:, 0, bass.ds(i * UW + half * HB, HB)], acc[half][:, :], ACT.Copy)
                ins.then_inc(blk_act, 1)
            nxt[0] += IN_FULL * KC
            end = SEG["eo"][0]
            hi_until(end + 1)
            block_out(end, [(proj[:, 0, IN_FULL * UW:], acc[0][:, :])])
            heads_out(0, NH0, lambda k: qk_t[:, k, :])
            act.wait_ge(blk_act, IN_FULL + 1)
            act.wait_ge(blk_dve, IN_FULL + 1)
            for t in range(TT):
                ins = act.activation(proj[:, t, COL_RG:], proj[:, t, COL_RG:], ACT.Silu)
            ins.then_inc(swish, 1)
            softmax("moba", MOBA_H, sc0, pr0, row0, MOBA_D ** -0.5)
            act.wait_ge(cen_ready, 1)
            act.activation(tmp0[:].rearrange("p k n -> p (k n)")[:, 0:TT * RET_V_W],
                           xn0[:].rearrange("p t n -> p (t n)"), ACT.Square).then_inc(var_ready, 1)
            act.wait_ge(vsum_ready, 1)
            act.activation(gns[:, 2], gns[:, 1], ACT.Sqrt, bias=eps, scale=1.0 / RET_DV).then_inc(var_ready, 1)
            turn("cat")
            hi_until(SEG["q0"][0] + 1)
            squares(1, [(h[:, t, :], xn0[:, t, :]) for t in range(TT)], [D] * TT)
            turn("ffn0")
            peer(0)
            squares(2, [(h[:, t, :], xn1[:, t, :]) for t in range(TT)], [D] * TT)
            turn("attn1")
            end = SEG["uq"][0]
            hi_until(end + 1)
            block_out(end, [(down[:, 0, k * (MLA_DOWN // 2):(k + 1) * (MLA_DOWN // 2)], acc[k][:, 0:MLA_DOWN // 2])
                            for k in range(2)])
            squares(3, [(down[:, t, a:a + n], xn1[:, t, a:a + n]) for a, n in ((0, Q_RANK), (Q_RANK, KV_RANK))
                        for t in range(TT)], [Q_RANK] * TT + [KV_RANK] * TT)
            turn("down")
            col = 0
            for seg, dst in (("uq", q1), ("ukv", kv)):
                col = 0
                for units, halves in blocks_of(seg):
                    end = units[-1][0] + 1
                    hi_until(end + 1)
                    block_out(end, [(dst[:, 0, col + k * HB:col + (k + 1) * HB], acc[k][:, :]) for k in range(len(halves))])
                    col += len(halves) * HB
            heads_out(HD0, 2 * MLA_H, lambda k: q_t[:, k, :] if k < MLA_H else k_t[:, k - MLA_H, :])
            softmax("mla", MLA_H, sc1, pr1, row1, MLA_QD ** -0.5)
            turn("heads")
            hi_until(SEG["q1"][0] + 1)
            squares(4, [(h[:, t, :], xn1[:, t, :]) for t in range(TT)], [D] * TT)
            turn("ffn1")
            peer(1)
            squares(5, [(h[:, t, :], fin[:, t, :]) for t in range(TT)], [D] * TT)

        @block.vector
        def _(dve):
            nxt = [0]
            own = [0]
            count = {}

            def tick(ins):
                ins.then_inc(dve_step, 1)
                own[0] += 1

            def settle(at=0):
                dve.wait_ge(dve_step, own[0] + at)
                if not isinstance(at, int):
                    dve.memset(stat[:, 0:1], 0.0)

            def then(ins, at=0):
                tick(ins)
                settle(at)

            def lo(u, at=0):
                dve.wait_ge(hi_ready, u + 1 + at)
                dve.tensor_tensor(w_lo[:, u % SPLITS, :], raw[:, u % RING, :], w_hi[:, u % SPLITS, :].bitcast(F32),
                                  ALU.subtract).then_inc(lo_ready, 1)

            def lo_until(u):
                while nxt[0] < min(u, N_UNITS):
                    lo(nxt[0])
                    nxt[0] += 1

            def turn(name):
                at, c0, n, g = TURN_AT[name]
                for c in range(n + 1):
                    if c < n:
                        dve.wait_ge(turn_ps, at + c + 1)
                        if at + c >= FLIGHT:
                            dve.wait_ge(turn_lo, at + c - FLIGHT + 1)
                        src, dst = trn[(at + c) % 2][:, 0:SEQ], xt_f[:, (at + c) % FLIGHT, :]
                        if g is None:
                            ins = dve.tensor_copy(dst, src)
                        else:
                            ins = dve.tensor_scalar(dst, src, gain[:, g + c:g + c + 1], None, ALU.mult)
                        ins.then_inc(turn_f, 1)
                    if c:
                        m = c - 1
                        dve.wait_ge(turn_hi, at + m + 1)
                        hi_t, lo_t = xt(c0 + m)
                        dve.tensor_tensor(lo_t, xt_f[:, (at + m) % FLIGHT, :], hi_t.bitcast(F32),
                                          ALU.subtract).then_inc(turn_lo, 1)

            def normed(n_at, rows, name):
                dve.wait_ge(sq_ready, n_at + 1)
                then(dve.reciprocal(stat[:, 0:len(rows)], stat[:, 4:4 + len(rows)]))
                for k, (dst, src) in enumerate(rows):
                    ins = dve.tensor_scalar(dst, src, stat[:, k:k + 1], None, ALU.mult)
                ins.then_inc(src_ready, 1)

            def block_out(n, dests):
                dve.wait_ge(unit_used, n)
                for dst, src in dests:
                    ins = dve.tensor_copy(dst, src)
                ins.then_inc(blk_dve, 1)

            def residual(n, ms):
                dve.wait_ge(unit_used, n)
                for t in range(TT):
                    for half in range(2):
                        hs = h[:, t, half * HB:(half + 1) * HB]
                        ins = dve.tensor_tensor(hs, acc[2 * t + half][:, :], hs, ALU.add)
                ins.then_inc(ms_ready, 1)

            def rope(xv, heads, r2, tab, tmp):
                cos, sin = table(tab, r2)
                sh = [P, TT, heads, r2]
                cb, sb_ = spread(cos, sh, 2), spread(sin, sh, 2)
                x1, x2 = xv[:, :, :, 0:r2], xv[:, :, :, r2:2 * r2]
                t = [tmp[:, k, 0:TT * heads * r2].rearrange("p (t h r) -> p t h r", t=TT, h=heads) for k in range(4)]
                dve.tensor_tensor(t[0], x1, cb, ALU.mult)
                dve.tensor_tensor(t[1], x2, sb_, ALU.mult)
                dve.tensor_tensor(t[2], x2, cb, ALU.mult)
                then(dve.tensor_tensor(t[3], x1, sb_, ALU.mult))
                dve.tensor_tensor(x1, t[0], t[1], ALU.subtract)
                return dve.tensor_tensor(x2, t[2], t[3], ALU.add)

            def heads_out(at, n, dst):
                for k in range(1, n, 2):
                    dve.wait_ge(hd_ps, at + k + 1)
                    dve.tensor_copy(dst(k), trn[k % 2][0:dst(k).shape[0], 0:SEQ]).then_inc(hd_dve, 1)

            def attend(name, heads, sc, pt, row, scale):
                at, pa = QK_AT[name], PR_AT[name]
                mask = cst[:, C_MASK:C_MASK + 3 * P]
                for s in range(heads + 1):
                    if s < heads:
                        dve.wait_ge(qk_ps, at + s + 1)
                        if pa + s >= 2:
                            dve.wait_ge(probs, pa + s - 1)
                        for t, (a, b) in enumerate(((0, P), (P, 3 * P))):
                            ins = dve.tensor_tensor_reduce(sc[:, s % 2, a:b], sco[s % 2][:, a:b], mask[:, a:b], 1.0, -3.0e38,
                                                           ALU.add, ALU.max, row[:, 0, t, s:s + 1])
                        then(ins)
                        dve.tensor_scalar(row[:, 1, :, s], row[:, 0, :, s], -scale, None, ALU.mult).then_inc(masked, 1)
                    if s:
                        n = s - 1
                        dve.wait_ge(pt_ps, pa + n + 1)
                        if pa + n >= 2:
                            dve.wait_ge(pv_done, at + n - 1)
                        dve.tensor_copy(pt[:, n % 2, :], trn[n % 2][:, 0:3 * P]).then_inc(pt_ready, 1)

            def outputs(name, heads, row, dst):
                dve.wait_ge(pv_done, QK_AT[name] + heads)
                dve.wait_ge(probs, PR_AT[name] + heads)
                then(dve.reciprocal(row[:, 3], row[:, 2]))
                for t in range(TT):
                    for b in range(heads // 8):
                        ins = dve.tensor_tensor(dst[:, t, b * HB:(b + 1) * HB].rearrange("p (h d) -> p h d", h=8),
                                                acc[2 * t + b][:, :].rearrange("p (h d) -> p h d", h=8),
                                                spread(row[:, 3, t, 8 * b:8 * b + 8], [P, 8, 64], 2), ALU.mult)
                return ins

            def rank(values, out_v, out_n, at):
                then(dve.max(out_v[:, 0:8], values), at)
                dve.max_index(out_n[:, 0:8], out_v[:, 0:8], values)
                then(dve.match_replace(values, out_v[:, 0:8], values, LOWEST), at)
                then(dve.max(out_v[:, 8:16], values), at)
                then(dve.max_index(out_n[:, 8:16], out_v[:, 8:16], values), at)

            def peer(layer):
                u0, n = SEG[f"q{layer}"]
                lo_until(u0 + n + 1)
                for g in range(LISTS // 4):
                    dve.wait_ge(s_ps, layer * (LISTS // 4) + g + 1)
                    k = g // 2 * 8 + g % 2
                    dve.tensor_copy(scores[:, k:k + 7:2, :],
                                    trn[g % 2][:, :].rearrange("p (a n) -> p a n", a=4)).then_inc(s_rd, 1)
                dve.wait_ge(s_rd, (layer + 1) * (LISTS // 4))
                u0, n = SEG[f"u{layer}"]
                STEPS = 2 * 6
                start = own[0]
                with dve.Fori(0, n // 2 // RING) as i:
                    for k in range(RING):
                        lo(u0 + k + 1, i * RING)
                        if k % 2:
                            j = k // 2
                            then(dve.tensor_copy(lst[:], scores[:, i * 2 + j, :]), i * STEPS)
                            rank(lst[:], v16[:], n16[:, 0, :], i * STEPS)
                            dve.tensor_copy(best[:, i * 2 + j, :], v16[:])
                            tick(dve.tensor_copy(best_i[:, i * 2 + j, :], n16[:, 0, :]))
                assert own[0] - start == STEPS
                own[0] = start + STEPS * (n // 2 // RING)
                dve.wait_ge(dve_step, own[0])
                dve.drain().then_inc(listed, 1)
                STEPS = 10
                start = own[0]
                with dve.Fori(0, n // 2 // RING) as i:
                    at = i * STEPS
                    for k in range(RING):
                        lo(u0 + n // 2 + k + 1, i * RING)
                        if k == 0:
                            sh = [P, TOPK, TOPK]
                            then(dve.tensor_tensor(cand[:], spread(best[:, i * 2, :], sh, 2),
                                                   spread(best[:, i * 2 + 1, :], sh, 1), ALU.add), at)
                            rank(cand[:].rearrange("p a b -> p (a b)"), v16[:], n16[:, 0, :], at)
                        if k == 2:
                            dve.tensor_copy(tops[:, i, :], v16[:])
                            dve.tensor_scalar(n16[:, 1, :], n16[:, 0, :], 4, None, ALU.logical_shift_right)
                            then(dve.tensor_scalar(n16[:, 2, :], n16[:, 0, :], 15, None, ALU.bitwise_and), at)
                            then(dve.tensor_copy(f16[:], n16[:, 1:3, :]), at)
                            for q in range(2):
                                ins = dve.tensor_tensor(eqs[:, q], spread(f16[:, q, :], sh, 2), spread(iota16, sh, 1),
                                                        ALU.is_equal)
                            then(ins, at)
                            for q in range(2):
                                ins = dve.tensor_tensor(eqs[:, q], eqs[:, q], spread(best_i[:, i * 2 + q, :], sh, 1),
                                                        ALU.mult)
                            then(ins, at)
                            for q in range(2):
                                ins = dve.tensor_reduce(picks[:, q, i, :], eqs[:, q], AX_X, ALU.add)
                            then(ins, at)
                assert own[0] - start == STEPS, own[0] - start
                own[0] = start + STEPS * (n // 2 // RING)
                dve.wait_ge(dve_step, own[0])
                nxt[0] += n
                then(dve.tensor_copy(gsum[:, 0, :], tops[:, :, 0]))
                dve.tensor_tensor(tops[:], tops[:], spread(gsum[:, 0, :], [P, HEADS, TOPK], 2),
                                  ALU.subtract).then_inc(shifted, 1)
                dve.wait_ge(expd, layer + 1)
                then(dve.tensor_reduce(gsum[:, 0, :], tops[:], AX_X, ALU.add))
                then(dve.reciprocal(gsum[:, 1, :], gsum[:, 0, :]))
                dve.tensor_tensor(picks[:, 2], tops[:], spread(gsum[:, 1, :], [P, HEADS, TOPK], 2),
                                  ALU.mult).then_inc(gated, 1)
                for q in range(3):
                    dve.wait_ge(pk_ps, 3 * layer + q + 1)
                    dve.tensor_copy(pick_t[:, q, :], trn[q % 2][:, 0:SEQ]).then_inc(pk_rd, 1)
                dve.wait_ge(pk_rd, 3 * layer + 3)
                g0 = layer * (SEQ // 4)

                def hots(i, k):
                    dve.tensor_scalar(hot2[:, k % 8, :], iota, pick_t[:, 1, bass.ds(i + k, 1)], None, ALU.is_equal)
                    dve.tensor_scalar(hot1[:, k % 8, :], iota, pick_t[:, 0, bass.ds(i + k, 1)],
                                      pick_t[:, 2, bass.ds(i + k, 1)], ALU.is_equal, ALU.mult).then_inc(hot_ready, 1)

                def into_a(i, k):
                    at = a_t[:, :, bass.ds(i, 4)].rearrange("p n t -> p t n")
                    dve.tensor_tensor(at, trn[k][:, :].rearrange("p (t n) -> p t n", t=4), at, ALU.mult).then_inc(g_rd, 1)

                for k in range(8):
                    hots(0, k)
                with dve.Fori(0, SEQ // 8 - 1) as i:
                    for k in range(2):
                        dve.wait_ge(g_ps, i * 2 + (g0 + k + 1))
                        into_a(i * 8 + 4 * k, k)
                        for m in range(4):
                            hots(i * 8, 8 + 4 * k + m)
                for k in range(2):
                    dve.wait_ge(g_ps, g0 + SEQ // 4 - 1 + k)
                    into_a(SEQ - 8 + 4 * k, k)
                u0, n = SEG[f"v{layer}"]
                dve.wait_ge(g_rd, (layer + 1) * (SEQ // 4))

                def rest(i, k):
                    dve.wait_ge(ga_hi_ready, i + (layer * NKEYS + k + 1))
                    dve.tensor_tensor(ga_lo[:, k % 2, :], a_t[:, i + k, :], ga_hi[:, k % 2, :].bitcast(F32),
                                      ALU.subtract).then_inc(ga_lo_ready, 1)

                with dve.Fori(0, n // RING - 1) as i:
                    for k in range(RING):
                        rest(i * RING, k)
                        lo(u0 + k + 1, i * RING)
                nxt[0] += n - RING
                for k in range(n - RING, n):
                    rest(0, k)
                    lo_until(u0 + k + 2)
                residual(u0 + n, None)

            dve.wait_ge(s_cst, 48)
            dve.tensor_copy(stat[:, 0:1], eps).then_inc(ms_ready, 1)
            normed(0, [(xn0[:, t, :], h[:, t, :]) for t in range(TT)], "attn0")
            lo_until(1)
            turn("attn0")
            with dve.Fori(0, IN_FULL) as i:
                for k in range(KC):
                    lo(k + 1, i * KC)
                dve.wait_ge(unit_used, i * KC + KC)
                for half in range(2):
                    ins = dve.tensor_copy(proj[:, 1, bass.ds(i * UW + half * HB, HB)], acc[2 + half][:, :])
                ins.then_inc(blk_dve, 1)
            nxt[0] += IN_FULL * KC
            end = SEG["eo"][0]
            lo_until(end + 1)
            block_out(end, [(proj[:, 1, IN_FULL * UW:], acc[2][:, :])])
            dve.wait_ge(blk_act, IN_FULL + 1)
            dve.wait_ge(blk_dve, IN_FULL + 1)
            view = proj[:, :, 0:COL_MV].rearrange("p t (h d) -> p t h d", d=MOBA_D)
            rope(view, 2 * MOBA_H, MOBA_ROT // 2, C_MROPE, tmp0[:]).then_inc(roped, 1)
            dve.wait_ge(roped, 1)
            view = proj[:, :, COL_RQ:COL_RV].rearrange("p t (h d) -> p t h d", d=RET_DK)
            rope(view, 2 * RET_H, RET_DK // 2, C_RROPE, tmp0[:]).then_inc(roped, 1)
            heads_out(0, NH0, lambda k: qk_t[:, k, :])
            attend("moba", MOBA_H, sc0, pt0, row0, MOBA_D ** -0.5)
            outputs("moba", MOBA_H, row0, cat).then_inc(o_read, 1)
            dve.wait_ge(s_dec, 32)
            for n in range(RET_H):
                dve.wait_ge(qk_ps, QK_AT["ret"] + n + 1)
                if n >= 2:
                    dve.wait_ge(pv_done, QK_AT["ret"] + n - 1)
                dve.tensor_tensor(sc0[:, n % 2, 0:SEQ], sco[n % 2][:, 0:SEQ], dec[:, n, :], ALU.mult)
                dve.tensor_tensor(sc0[:, n % 2, SEQ:SEQ + P], sco[n % 2][:, SEQ:SEQ + P], dec[:, n, 0:P],
                                  ALU.mult).then_inc(masked, 1)
            dve.wait_ge(pv_done, QK_AT["ret"] + RET_H)
            for b in range(4):
                ins = dve.tensor_reduce(gns[:, 0, b // 2, 4 * (b % 2):4 * (b % 2) + 4],
                                        acc[b][:, :].rearrange("p (h d) -> p h d", h=4), AX_X, ALU.add)
            then(ins)
            then(dve.tensor_scalar(gns[:, 0], gns[:, 0], 1.0 / RET_DV, None, ALU.mult))
            for b in range(4):
                ins = dve.tensor_tensor(xn0[:, b // 2, HB * (b % 2):HB * (b % 2 + 1)].rearrange("p (h d) -> p h d", h=4),
                                        acc[b][:, :].rearrange("p (h d) -> p h d", h=4),
                                        spread(gns[:, 0, b // 2, 4 * (b % 2):4 * (b % 2) + 4], [P, 4, RET_DV], 2),
                                        ALU.subtract)
            ins.then_inc(cen_ready, 1)
            dve.wait_ge(var_ready, 1)
            dve.tensor_reduce(gns[:, 1], tmp0[:].rearrange("p k n -> p (k n)")[:, 0:TT * RET_V_W].rearrange(
                "p (t h d) -> p t h d", t=TT, h=RET_H), AX_X, ALU.add).then_inc(vsum_ready, 1)
            dve.wait_ge(swish, 1)
            for t in range(TT):
                ins = dve.tensor_tensor(proj[:, t, COL_RG:], proj[:, t, COL_RG:], gnb[:], ALU.mult)
            tick(ins)
            dve.wait_ge(var_ready, 2)
            then(dve.reciprocal(gns[:, 3], gns[:, 2]))
            for t in range(TT):
                ins = dve.tensor_tensor(xn0[:, t, :].rearrange("p (h d) -> p h d", h=RET_H),
                                        xn0[:, t, :].rearrange("p (h d) -> p h d", h=RET_H),
                                        spread(gns[:, 3, t, :], [P, RET_H, RET_DV], 2), ALU.mult)
            then(ins)
            for t in range(TT):
                ins = dve.tensor_tensor(cat[:, t, MOBA_W:], xn0[:, t, :], proj[:, t, COL_RG:], ALU.mult)
            ins.then_inc(src_ready, 1)
            turn("cat")
            lo_until(SEG["q0"][0] + 1)
            residual(SEG["q0"][0], None)
            normed(1, [(xn0[:, t, :], h[:, t, :]) for t in range(TT)], "ffn0")
            turn("ffn0")
            peer(0)

            normed(2, [(xn1[:, t, :], h[:, t, :]) for t in range(TT)], "attn1")
            turn("attn1")
            end = SEG["uq"][0]
            lo_until(end + 1)
            block_out(end, [(down[:, 1, k * (MLA_DOWN // 2):(k + 1) * (MLA_DOWN // 2)], acc[2 + k][:, 0:MLA_DOWN // 2])
                            for k in range(2)])
            dve.wait_ge(blk_act, IN_FULL + 2)
            dve.wait_ge(blk_dve, IN_FULL + 2)
            dve.tensor_copy(stat[:, 0:1], eps).then_inc(ms_ready, 1)
            view = down[:, :, Q_RANK + KV_RANK:].rearrange("p t (h d) -> p t h d", h=1)
            then(rope(view, 1, MLA_ROPE // 2, C_LROPE, tmp1[:]))
            ranges = [(t, a, n) for a, n in ((0, Q_RANK), (Q_RANK, KV_RANK)) for t in range(TT)]
            normed(3, [(xn1[:, t, a:a + n], down[:, t, a:a + n]) for t, a, n in ranges], "down")
            for t in range(TT):
                tick(dve.tensor_copy(kf[:, t, :].rearrange("p (h d) -> p h d", h=MLA_H)[:, :, MLA_NOPE:],
                                     spread(down[:, t, Q_RANK + KV_RANK:], [P, MLA_H, MLA_ROPE], 1)))
            turn("down")
            for seg, dst in (("uq", q1), ("ukv", kv)):
                col = 0
                for units, halves in blocks_of(seg):
                    end = units[-1][0] + 1
                    lo_until(end + 1)
                    block_out(end, [(dst[:, 1, col + k * HB:col + (k + 1) * HB], acc[2 + k][:, :])
                                    for k in range(len(halves))])
                    col += len(halves) * HB
            dve.wait_ge(blk_act, IN_FULL + 6)
            dve.wait_ge(blk_dve, IN_FULL + 6)
            view = q1[:].rearrange("p t (h d) -> p t h d", h=MLA_H)[:, :, :, MLA_NOPE:]
            rope(view, MLA_H, MLA_ROPE // 2, C_LROPE, tmp1[:]).then_inc(roped, 1)
            for t in range(TT):
                ins = dve.tensor_copy(kf[:, t, :].rearrange("p (h d) -> p h d", h=MLA_H)[:, :, 0:MLA_NOPE],
                                      kv[:, t, :].rearrange("p (h d) -> p h d", h=MLA_H)[:, :, 0:MLA_NOPE])
            ins.then_inc(roped, 1)
            heads_out(HD0, 2 * MLA_H, lambda k: q_t[:, k, :] if k < MLA_H else k_t[:, k - MLA_H, :])
            attend("mla", MLA_H, sc1, pt1, row1, MLA_QD ** -0.5)
            outputs("mla", MLA_H, row1, o1).then_inc(src_ready, 1)
            turn("heads")
            lo_until(SEG["q1"][0] + 1)
            residual(SEG["q1"][0], None)
            normed(4, [(xn1[:, t, :], h[:, t, :]) for t in range(TT)], "ffn1")
            turn("ffn1")
            peer(1)

            dve.wait_ge(sq_ready, 6)
            then(dve.reciprocal(stat[:, 0:TT], stat[:, 4:4 + TT]))
            dve.wait_ge(s_fing, 16)
            for t in range(TT):
                ins = dve.scalar_tensor_tensor(fin[:, t, :], h[:, t, :], stat[:, t:t + 1], fing[:], ALU.mult, ALU.mult)
            ins.then_inc(src_ready, 1)

        @block.tensor
        def _(pe):
            def split_ready(u, at=0):
                pe.wait_ge(lo_ready, u + 1 + at)

            def unit(u, parts, halves, start, stop, at=0):
                split_ready(u, at)
                hi_u, lo_u = w_hi[:, u % SPLITS, :], w_lo[:, u % SPLITS, :]
                for p, (c, off) in enumerate(parts):
                    xh, xl = xt(c)
                    col = off
                    for half, width in enumerate(halves):
                        for t in range(TT):
                            dst = acc[2 * t + half][:, 0:width]
                            th, tl = xh[:, t * P:(t + 1) * P], xl[:, t * P:(t + 1) * P]
                            first, last = start and p == 0, stop and p == len(parts) - 1
                            pe.matmul(dst, th, hi_u[:, col:col + width], start=first, stop=False)
                            pe.matmul(dst, tl, hi_u[:, col:col + width], start=False, stop=False)
                            ins = pe.matmul(dst, th, lo_u[:, col:col + width], start=False, stop=last)
                        col += width
                ins.then_inc(unit_used, 1)

            blocks = [0]

            def project(seg):
                for units, halves in blocks_of(seg):
                    if blocks[0]:
                        pe.wait_ge(blk_act, blocks[0])
                        pe.wait_ge(blk_dve, blocks[0])
                    for n, (u, parts) in enumerate(units):
                        unit(u, parts, halves, n == 0, n == len(units) - 1)
                    blocks[0] += 1

            def turn(name, src):
                at, _, n, _ = TURN_AT[name]
                pe.wait_ge(src_ready, TURN_NO[name] + 1)
                for c in range(n):
                    if at + c >= 2:
                        pe.wait_ge(turn_f, at + c - 1)
                    for t in range(TT):
                        ins = pe.transpose(trn[(at + c) % 2][:, t * P:(t + 1) * P], src[:, t, c * P:(c + 1) * P], ident)
                    ins.then_inc(turn_ps, 1)
                pe.wait_ge(turn_lo, at + n)

            def turn_heads(at, n, src, width):
                for k in range(n):
                    if at + k >= 2:
                        pe.wait_ge(hd_dve if k % 2 else hd_act, (at + k) // 2)
                    for t in range(TT):
                        ins = pe.transpose(trn[k % 2][0:width, t * P:(t + 1) * P], src(k, t), ident)
                    ins.then_inc(hd_ps, 1)
                pe.wait_ge(hd_act, (at + n) // 2)
                pe.wait_ge(hd_dve, (at + n) // 2)

            def attend(name, heads, q, k, v, pr, pt):
                at, pa = QK_AT[name], PR_AT[name]
                for s in range(heads + 2):
                    if s < heads:
                        if at + s >= 2:
                            pe.wait_ge(masked, at + s - 1)
                        pe.matmul(sco[s % 2][:, 0:P], q(s)[:, 0:P], k(s)[:, 0:P], start=True, stop=True)
                        pe.matmul(sco[s % 2][:, P:3 * P], q(s)[:, P:SEQ], k(s), start=True, stop=True).then_inc(qk_ps, 1)
                    if 1 <= s <= heads:
                        n = s - 1
                        pe.wait_ge(probs, pa + n + 1)
                        if pa + n >= 2:
                            pe.wait_ge(pt_ready, pa + n - 1)
                        for b in range(3):
                            ins = pe.transpose(trn[n % 2][:, b * P:(b + 1) * P], pr[:, n % 2, b * P:(b + 1) * P], ident)
                        ins.then_inc(pt_ps, 1)
                    if s >= 2:
                        n = s - 2
                        pe.wait_ge(pt_ready, pa + n + 1)
                        cols = slice((n % 8) * 64, (n % 8) * 64 + 64)
                        o0, o1_ = acc[n // 8][:, cols], acc[2 + n // 8][:, cols]
                        pe.matmul(o0, pt[:, n % 2, 0:P], v(n, 0), start=True, stop=True)
                        pe.matmul(o1_, pt[:, n % 2, P:2 * P], v(n, 0), start=True, stop=False)
                        pe.matmul(o1_, pt[:, n % 2, 2 * P:], v(n, 1), start=False, stop=True).then_inc(pv_done, 1)

            def turned_unit(u, bank, at=0):
                split_ready(u, at)
                dst = sco[bank][:, 0:SEQ]
                for c in range(KC):
                    wh, wl = w_hi[:, u % SPLITS, c * P:(c + 1) * P], w_lo[:, u % SPLITS, c * P:(c + 1) * P]
                    xh, xl = xt(c)
                    pe.matmul(dst, wh, xh, start=(c == 0), stop=False)
                    pe.matmul(dst, wl, xh, start=False, stop=False)
                    ins = pe.matmul(dst, wh, xl, start=False, stop=(c == KC - 1))
                ins.then_inc(unit_used, 1)

            def peer(layer):
                b = layer * (PEER_H + NKEYS)
                u0, n = SEG[f"q{layer}"]
                for k in range(n):
                    if b + k >= 2:
                        pe.wait_ge(a_read, b + k - 1)
                    turned_unit(u0 + k, k % 2)
                b += n
                pe.wait_ge(s_keys, 16 * (layer + 1))
                pe.wait_ge(a_read, b)
                g0 = layer * (LISTS // 4)
                for g in range(LISTS // 4):
                    if g >= 2:
                        pe.wait_ge(s_rd, g0 + g - 1)
                    for m in range(4):
                        t, hh, half = g // 4, g // 2 % 2 * 4 + m, g % 2
                        rows = slice(64 * half, 64 * half + 64)
                        ins = pe.matmul(trn[g % 2][:, m * P:(m + 1) * P], qry_t[rows, hh, t * P:(t + 1) * P],
                                        kys[rows, hh, :], start=True, stop=True)
                    ins.then_inc(s_ps, 1)
                u0, n = SEG[f"u{layer}"]
                with pe.Fori(0, n // RING) as i:
                    for k in range(RING):
                        pe.wait_ge(a_read, i * RING + (b + k - 1))
                        turned_unit(u0 + k, k % 2, i * RING)
                pe.wait_ge(gated, layer + 1)
                for q in range(3):
                    if q == 2:
                        pe.wait_ge(pk_rd, 3 * layer + 1)
                    for t in range(TT):
                        ins = pe.transpose(trn[q % 2][:, t * P:(t + 1) * P],
                                           picks[:, q, t * PEER_H:(t + 1) * PEER_H, :].rearrange("p h k -> p (h k)"), ident)
                    ins.then_inc(pk_ps, 1)
                g0 = layer * (SEQ // 4)

                def gates(i, k, bank):
                    for m in range(4):
                        pe.wait_ge(hot_ready, i * 4 + (4 * (g0 + k) + m + 1))
                        ins = pe.matmul(trn[bank][:, m * P:(m + 1) * P], hot2[:, 4 * bank + m, :], hot1[:, 4 * bank + m, :], start=True, stop=True)
                    ins.then_inc(g_ps, 1)

                pe.wait_ge(pk_rd, 3 * layer + 3)
                gates(0, 0, 0)
                gates(0, 1, 1)
                with pe.Fori(0, SEQ // 8 - 1) as i:
                    for k in range(2):
                        pe.wait_ge(g_rd, i * 2 + (g0 + k + 1))
                        gates(i * 2, 2 + k, k)
                u0, n = SEG[f"v{layer}"]

                def expert_unit(i, k, start, stop):
                    pe.wait_ge(ga_lo_ready, i + (layer * NKEYS + k + 1))
                    split_ready(u0 + k, i)
                    hi_u, lo_u = w_hi[:, (u0 + k) % SPLITS, :], w_lo[:, (u0 + k) % SPLITS, :]
                    for half in range(2):
                        for t in range(TT):
                            dst = acc[2 * t + half][:, :]
                            ah, al = ga_hi[:, k % 2, t * P:(t + 1) * P], ga_lo[:, k % 2, t * P:(t + 1) * P]
                            cols = slice(half * HB, (half + 1) * HB)
                            pe.matmul(dst, ah, hi_u[:, cols], start=start, stop=False, skip_group_check=True)
                            pe.matmul(dst, al, hi_u[:, cols], start=False, stop=False, skip_group_check=True)
                            ins = pe.matmul(dst, ah, lo_u[:, cols], start=False, stop=stop, skip_group_check=True)
                    ins.then_inc(unit_used, 1)

                for k in range(RING):
                    expert_unit(0, k, k == 0, False)
                with pe.Fori(0, n // RING - 2) as i:
                    for k in range(RING):
                        expert_unit(i * RING, RING + k, False, False)
                for k in range(n - RING, n):
                    expert_unit(0, k, False, k == n - 1)

            pe.wait_ge(s_cst, 48)
            turn("attn0", xn0)
            for k in range(KC):
                unit(k, [(k, 0)], [HB, HB], k == 0, k == KC - 1)
            with pe.Fori(1, IN_FULL) as i:
                pe.wait_ge(blk_act, i)
                pe.wait_ge(blk_dve, i)
                for k in range(KC):
                    unit(k, [(k, 0)], [HB, HB], k == 0, k == KC - 1, i * KC)
            blocks[0] = IN_FULL
            project("in")
            pe.wait_ge(roped, 2)
            pe.wait_ge(blk_act, blocks[0])
            pe.wait_ge(blk_dve, blocks[0])
            cols = [0, MOBA_W, COL_RQ, COL_RQ + RET_QK_W]
            turn_heads(0, NH0, lambda k, t: proj[:, t, cols[k // 4] + (k % 4) * P:cols[k // 4] + (k % 4 + 1) * P], P)

            def pair(base):
                return lambda n: qk_t[64 * (n % 2):64 * (n % 2) + 64, base + n // 2, :]

            attend("moba", MOBA_H, pair(0), pair(4), lambda n, t: proj[:, t, COL_MV + n * 64:COL_MV + (n + 1) * 64], pr0, pt0)
            pe.wait_ge(o_read, 1)
            at = QK_AT["ret"]
            for s in range(RET_H + 1):
                if s < RET_H:
                    pe.wait_ge(masked, at + s - 1)
                    q, k = pair(8)(s), pair(12)(s)
                    pe.matmul(sco[s % 2][:, 0:SEQ], k[:, 0:P], q, start=True, stop=True)
                    pe.matmul(sco[s % 2][:, SEQ:SEQ + P], k[:, P:SEQ], q[:, P:SEQ], start=True, stop=True).then_inc(qk_ps, 1)
                if s:
                    n = s - 1
                    pe.wait_ge(masked, at + n + 1)
                    c = slice((n % 4) * RET_DV, (n % 4 + 1) * RET_DV)
                    v = [proj[:, t, COL_RV + n * RET_DV:COL_RV + (n + 1) * RET_DV] for t in range(TT)]
                    pe.matmul(acc[n // 4][:, c], sc0[:, n % 2, 0:P], v[0], start=True, stop=True)
                    pe.matmul(acc[2 + n // 4][:, c], sc0[:, n % 2, P:SEQ], v[0], start=True, stop=False)
                    pe.matmul(acc[2 + n // 4][:, c], sc0[:, n % 2, SEQ:SEQ + P], v[1], start=False,
                              stop=True).then_inc(pv_done, 1)
            turn("cat", cat)
            blocks[0] = 0
            project("eo")
            turn("ffn0", xn0)
            peer(0)
            turn("attn1", xn1)
            blocks[0] = 0
            project("down")
            blocks[0] = IN_FULL + 2
            turn("down", xn1)
            project("uq")
            project("ukv")
            pe.wait_ge(roped, 4)
            pe.wait_ge(blk_act, blocks[0])
            pe.wait_ge(blk_dve, blocks[0])
            turn_heads(HD0, 2 * MLA_H, lambda k, t: (q1 if k < MLA_H else kf)[:, t, (k % MLA_H) * MLA_QD:(k % MLA_H + 1) * MLA_QD],
                       MLA_QD)
            attend("mla", MLA_H, lambda n: q_t[:, n, :], lambda n: k_t[:, n, :],
                   lambda n, t: kv[:, t, n * 128 + MLA_NOPE:(n + 1) * 128], pr1, pt1)
            turn("heads", o1)
            blocks[0] = 0
            project("oo")
            turn("ffn1", xn1)
            peer(1)


def kernel(**inputs):
    import numpy as _np
    import concourse.bacc as _bacc
    from concourse import mybir as _mybir
    from concourse.bass_utils import run_bass_kernel_spmd as _run

    a = {k: _np.asarray(v) for k, v in inputs.items()}

    def rows(m):
        return m.reshape(-1, P, UW)

    def halves(m):
        return m.reshape(-1, 2, P, HB).transpose(0, 2, 1, 3).reshape(-1, P, UW)

    def turned(m):
        return m.reshape(-1, P, KC, P).transpose(0, 3, 2, 1).reshape(-1, P, UW)

    def column(v):
        return v.reshape(-1, P).T

    w_in = a["ev_w_in"][0]
    full = IN_FULL * UW
    down = _np.zeros((D, UW), _np.float32)
    down[:, :MLA_DOWN] = a["od_w_down"][0]
    uq, ukv = a["od_w_uq"][0], a["od_w_ukv"][0]
    arrays = {
        "w_in": _np.concatenate([rows(w_in[:, k * UW:(k + 1) * UW]) for k in range(IN_FULL)] + [halves(w_in[:, full:])]),
        "w_eo": rows(a["ev_w_o"][0]),
        "w_down": rows(down),
        "w_uq": _np.concatenate([rows(uq[:, :UW]), halves(uq[:, UW:])]),
        "w_ukv": _np.concatenate([rows(ukv[:, :UW]), rows(ukv[:, UW:])]),
        "w_oo": rows(a["od_w_o"][0]),
    }
    for layer in range(2):
        arrays[f"w_q{layer}"] = turned(a["peer_wq"][layer].T)
        arrays[f"w_u{layer}"] = turned(a["peer_u"][layer])
        arrays[f"w_v{layer}"] = rows(a["peer_v"][layer])
    arrays["x"] = a["x"].reshape(TT, P, D).transpose(1, 0, 2)
    arrays["keys"] = a["peer_keys"].transpose(0, 2, 4, 1, 3).reshape(2, P, PEER_H, NKEYS)
    arrays["gains"] = _np.concatenate([column(a["attn_norm"][0]), column(a["ffn_norm"][0]), column(a["attn_norm"][1]),
                                       column(a["ffn_norm"][1]), column(a["od_q_norm"][0]), column(a["od_kv_norm"][0])], axis=1)
    arrays["gn_gain"] = a["ev_ret_gn"][0]
    arrays["fin_gain"] = a["final_norm"]
    arrays["consts"] = constants()
    arrays["decay"] = decay_table()
    arrays = {f"in_{k}_dram": _np.ascontiguousarray(v) for k, v in arrays.items()}

    nc = _bacc.Bacc("TRN2", target_bir_lowering=False, num_devices=1)
    t = {k[3:-5]: nc.dram_tensor(k, v.shape, _mybir.dt.from_np(v.dtype), kind="ExternalInput").ap() for k, v in arrays.items()}
    out = nc.dram_tensor("out_dram", (P, TT, D), _mybir.dt.float32, kind="ExternalOutput").ap()
    build(nc, t["x"], {k[2:]: v for k, v in t.items() if k.startswith("w_")}, t["keys"], t["gains"], t["gn_gain"],
          t["fin_gain"], t["consts"], t["decay"], out)
    r = _run(nc, [arrays], core_ids=[0])
    return r.results[0]["out_dram"].transpose(1, 0, 2).reshape(1, SEQ, D)
```

```python
from contextlib import ExitStack

import numpy as np

import concourse.bass as bass
from concourse import mybir

ALU = mybir.AluOpType
ACT = mybir.ActivationFunctionType
AX_X = mybir.AxisListType.X
F32 = mybir.dt.float32
F32R = mybir.dt.float32r
U32 = mybir.dt.uint32

P = 128
SEQ = 256
TT = SEQ // P
D = 1024
KC = D // P
EPS = 1e-6
ROPE_THETA, RET_THETA = 500000.0, 10000.0

MOBA_H, MOBA_D, MOBA_ROT = 8, 64, 16
RET_H, RET_DK, RET_DV = 8, 64, 128
MOBA_W, RET_QK_W, RET_V_W = MOBA_H * MOBA_D, RET_H * RET_DK, RET_H * RET_DV
COL_MV = 2 * MOBA_W
COL_RQ = 3 * MOBA_W
COL_RV = COL_RQ + 2 * RET_QK_W
COL_RG = COL_RV + RET_V_W
EVEN_IN = COL_RG + RET_V_W
EVEN_OUT = MOBA_W + RET_V_W
MLA_H, MLA_NOPE, MLA_ROPE, MLA_V = 16, 64, 32, 64
MLA_QD = MLA_NOPE + MLA_ROPE
Q_RANK, KV_RANK = 512, 256
MLA_DOWN = Q_RANK + KV_RANK + MLA_ROPE
PEER_H, NKEYS, TOPK = 8, 128, 16
NEXP = NKEYS * NKEYS
PICKS = PEER_H * TOPK
LISTS = TT * PEER_H * 2
HEADS = TT * PEER_H

UW = 1024
HB = 512
RING = 4
SPLITS = 4
HOTS = 4
LOWEST = -3.0e38

C_ID = 0
C_IOTA = C_ID + P
C_MASK = C_IOTA + P
C_MROPE = C_MASK + 3 * P
C_RROPE = C_MROPE + 2 * TT * (MOBA_ROT // 2)
C_LROPE = C_RROPE + 2 * TT * (RET_DK // 2)
C_EPS = C_LROPE + 2 * TT * (MLA_ROPE // 2)
C_END = C_EPS + 1

G_ATTN0, G_FFN0, G_ATTN1, G_FFN1 = 0, KC, 2 * KC, 3 * KC
G_Q = 4 * KC
G_KV = G_Q + Q_RANK // P
G_END = G_KV + KV_RANK // P


def rope_table(rot, theta):
    inv = (1.0 / (np.float32(theta) ** (np.arange(0, rot, 2, dtype=np.float32) / np.float32(rot)))).astype(np.float32)
    ang = np.arange(SEQ, dtype=np.float32)[:, None] * inv[None, :]
    cs = np.stack([np.cos(ang), np.sin(ang)]).astype(np.float32)
    return cs.reshape(2, TT, P, rot // 2).transpose(2, 0, 1, 3).reshape(P, -1)


def constants():
    tri = np.where(np.arange(P)[None, :] <= np.arange(P)[:, None], 0.0, -1.0e30)
    c = np.concatenate([np.eye(P), np.tile(np.arange(P), (P, 1)), tri, np.zeros((P, P)), tri,
                        rope_table(MOBA_ROT, ROPE_THETA), rope_table(RET_DK, RET_THETA),
                        rope_table(MLA_ROPE, ROPE_THETA), np.full((P, 1), EPS)], axis=1)
    assert c.shape[1] == C_END
    return c.astype(np.float32)


def decay_table():
    log_g = np.log(1.0 - 2.0 ** (-5.0 - np.arange(RET_H)))
    diff = np.arange(SEQ)[None, :] - np.arange(P)[:, None]
    d = np.where(diff[:, None, :] >= 0, np.exp(log_g[None, :, None] * np.maximum(diff, 0)[:, None, :]), 0.0)
    return (d * RET_DK ** -0.5).astype(np.float32)


IN_FULL = EVEN_IN // UW
SEG = {}
_at = 0
for _name, _n in (("in", IN_FULL * KC + KC // 2), ("eo", EVEN_OUT // P), ("q0", PEER_H), ("u0", NKEYS), ("v0", NKEYS),
                  ("down", KC), ("uq", 6), ("ukv", 4), ("oo", KC), ("q1", PEER_H), ("u1", NKEYS), ("v1", NKEYS)):
    SEG[_name] = (_at, _n)
    _at += _n
N_UNITS = _at

TURNS = (("attn0", 0, KC, G_ATTN0), ("cat", 0, EVEN_OUT // P, None), ("ffn0", 0, KC, G_FFN0),
         ("attn1", 0, KC, G_ATTN1), ("down", 0, (Q_RANK + KV_RANK) // P, G_Q), ("heads", 0, KC, None),
         ("ffn1", 0, KC, G_FFN1))
TURN_AT = {}
_at = 0
for _name, _c0, _n, _g in TURNS:
    TURN_AT[_name] = (_at, _c0, _n, _g)
    _at += _n
TURN_NO = {t[0]: i for i, t in enumerate(TURNS)}


def blocks_of(seg):
    u0, _ = SEG[seg]
    if seg == "in":
        first = u0 + IN_FULL * KC
        return [([(first + n, [(2 * n, 0), (2 * n + 1, HB)]) for n in range(KC // 2)], [HB])]
    if seg == "eo":
        return [([(u0 + c, [(c, 0)]) for c in range(EVEN_OUT // P)], [HB, HB])]
    if seg == "down":
        return [([(u0 + c, [(c, 0)]) for c in range(KC)], [MLA_DOWN // 2, MLA_DOWN // 2])]
    if seg == "uq":
        return [([(u0 + c, [(c, 0)]) for c in range(4)], [HB, HB]),
                ([(u0 + 4 + n, [(2 * n, 0), (2 * n + 1, HB)]) for n in range(2)], [HB])]
    if seg == "ukv":
        return [([(u0 + 2 * b + n, [(4 + n, 0)]) for n in range(2)], [HB, HB]) for b in range(2)]
    return [([(u0 + c, [(c, 0)]) for c in range(KC)], [HB, HB])]


def build(nc, x, w, peer_keys, gains, gn_gain, fin_gain, consts, decay, out):
    with ExitStack() as ctx:
        def sb(name, shape, dt=F32, scope=ctx):
            return scope.enter_context(nc.sbuf_tensor(name, shape, dt))

        def sem(name):
            return ctx.enter_context(nc.semaphore(name))

        cst = sb("cst", [P, C_END])
        gain = sb("gain", [P, G_END])
        h = sb("h", [P, TT, D])
        xt_hi = sb("xt_hi", [P, KC, SEQ], F32R)
        xt_lo = sb("xt_lo", [P, KC, SEQ], F32R)
        raw = sb("raw", [P, RING, UW])
        w_hi = sb("w_hi", [P, SPLITS, HB], F32R)
        w_lo = sb("w_lo", [P, SPLITS, HB], F32R)
        stat = sb("stat", [P, 8])
        picks = sb("picks", [P, 3, HEADS, TOPK])
        gsum = sb("gsum", [P, 2, HEADS])

        s0 = ExitStack()
        xn0 = sb("xn0", [P, TT, D], F32, s0)
        xt2_hi = sb("xt2_hi", [P, 4, SEQ], F32R, s0)
        xt2_lo = sb("xt2_lo", [P, 4, SEQ], F32R, s0)
        proj = sb("proj", [P, TT, EVEN_IN], F32, s0)
        qk_t = sb("qk_t", [P, 16, SEQ], F32, s0)
        dec = sb("dec", [P, RET_H, SEQ], F32, s0)
        cat = sb("cat", [P, TT, EVEN_OUT], F32, s0)
        sc0 = sb("sc0", [P, 2, 3 * P], F32, s0)
        pr0 = sb("pr0", [P, 2, 3 * P], F32, s0)
        pt0 = sb("pt0", [P, 2, 3 * P], F32, s0)
        row0 = sb("row0", [P, 6, TT, MOBA_H], F32, s0)
        tmp0 = sb("tmp0", [P, 4, TT * 16 * 32], F32, s0)
        gnb = sb("gnb", [P, RET_V_W], F32, s0)
        gns = sb("gns", [P, 4, TT, RET_H], F32, s0)
        s0.close()
        s1 = ExitStack()
        xn1 = sb("xn1", [P, TT, D], F32, s1)
        down = sb("down", [P, TT, MLA_DOWN], F32, s1)
        q1 = sb("q1", [P, TT, MLA_H * MLA_QD], F32, s1)
        kv = sb("kv", [P, TT, MLA_H * (MLA_NOPE + MLA_V)], F32, s1)
        kf = sb("kf", [P, TT, MLA_H * MLA_QD], F32, s1)
        q_t = sb("q_t", [MLA_QD, MLA_H, SEQ], F32, s1)
        k_t = sb("k_t", [MLA_QD, MLA_H, SEQ], F32, s1)
        sc1 = sb("sc1", [P, 2, 3 * P], F32, s1)
        pr1 = sb("pr1", [P, 2, 3 * P], F32, s1)
        pt1 = sb("pt1", [P, 2, 3 * P], F32, s1)
        row1 = sb("row1", [P, 6, TT, MLA_H], F32, s1)
        tmp1 = sb("tmp1", [P, 4, TT * MLA_H * 16], F32, s1)
        o1 = sb("o1", [P, TT, D], F32, s1)
        s1.close()
        s2 = ExitStack()
        a_t = sb("a_t", [P, NKEYS, SEQ], F32, s2)
        s3 = ExitStack()
        best = sb("best", [P, LISTS, TOPK], F32, s3)
        best_i = sb("best_i", [P, LISTS, TOPK], F32, s3)
        tops = sb("tops", [P, HEADS, TOPK], F32, s3)
        lst = sb("lst", [P, 2, NKEYS], F32, s3)
        v16 = sb("v16", [P, 2, TOPK], F32, s3)
        n16 = sb("n16", [P, 2, TOPK], U32, s3)
        nab = sb("nab", [P, 2, TOPK], U32, s3)
        junk = sb("junk", [P, 2], F32, s3)
        f16 = sb("f16", [P, 2, TOPK], F32, s3)
        cand = sb("cand", [P, TOPK, TOPK], F32, s3)
        eqs = sb("eqs", [P, 2, TOPK, TOPK], F32, s3)
        s3.close()
        s4 = ExitStack()
        pick_t = sb("pick_t", [P, 3, SEQ], F32, s4)
        hot2 = xt_lo[:].rearrange("p a b -> p (a b)").rearrange("p (k m n) -> p k m n", k=HOTS, m=4)
        hot1 = sb("hot1", [P, HOTS, 4, P], F32, s4)
        s4.close()
        s5 = ExitStack()
        ga_hi = sb("ga_hi", [P, 2, SEQ], F32R, s5)
        ga_lo = sb("ga_lo", [P, 2, SEQ], F32R, s5)
        s5.close()
        s2.close()
        s6 = ExitStack()
        fin = sb("fin", [P, TT, D], F32, s6)
        fing = sb("fing", [P, D], F32, s6)
        kys = sb("kys", [P, PEER_H, NKEYS], F32, s6)
        qry_t = sb("qry_t", [P, PEER_H, SEQ], F32, s6)
        s6.close()
        S_TILES = LISTS * NKEYS // SEQ
        scores = a_t[:, NKEYS - S_TILES:, :].rearrange("p a (b n) -> p (a b) n", n=NKEYS)

        acc = [ctx.enter_context(nc.psum_tensor(f"acc{i}", [P, HB], F32)) for i in range(4)]
        sco = [ctx.enter_context(nc.psum_tensor(f"sco{i}", [P, HB], F32)) for i in range(2)]
        trn = [ctx.enter_context(nc.psum_tensor(f"trn{i}", [P, HB], F32)) for i in range(2)]

        banks = [trn[0], sco[0], trn[1], sco[1]]

        s_cst = sem("s_cst")
        s_dec = sem("s_dec")
        s_keys = sem("s_keys")
        s_fing = sem("s_fing")
        s_out = sem("s_out")
        raw_in = [sem(f"raw_in{i}") for i in range(RING)]
        hi_ready = sem("hi_ready")
        lo_ready = sem("lo_ready")
        half_used = sem("half_used")
        act_step = sem("act_step")
        dve_step = sem("dve_step")
        src_ready = sem("src_ready")
        turn_ps = sem("turn_ps")
        turn_hi = sem("turn_hi")
        turn_lo = sem("turn_lo")
        sq_ready = sem("sq_ready")
        ms_ready = sem("ms_ready")
        blk_act = sem("blk_act")
        blk_dve = sem("blk_dve")
        roped = sem("roped")
        hd_ps = sem("hd_ps")
        hd_act = sem("hd_act")
        hd_dve = sem("hd_dve")
        qk_ps = sem("qk_ps")
        masked = sem("masked")
        probs = sem("probs")
        pt_ps = sem("pt_ps")
        pt_ready = sem("pt_ready")
        pv_done = sem("pv_done")
        o_read = sem("o_read")
        cen_ready = sem("cen_ready")
        var_ready = sem("var_ready")
        vsum_ready = sem("vsum_ready")
        swish = sem("swish")
        a_read = sem("a_read")
        s_ps = sem("s_ps")
        s_rd = sem("s_rd")
        listed = sem("listed")
        shifted = sem("shifted")
        expd = sem("expd")
        gated = sem("gated")
        pk_ps = sem("pk_ps")
        pk_rd = sem("pk_rd")
        hot_ready = sem("hot_ready")
        hot_gated = sem("hot_gated")
        g_ps = sem("g_ps")
        g_rd = sem("g_rd")
        ga_hi_ready = sem("ga_hi_ready")
        ga_lo_ready = sem("ga_lo_ready")

        ident = cst[:, C_ID:C_ID + P]
        iota = cst[:, C_IOTA:C_IOTA + P]
        iota16 = cst[:, C_IOTA:C_IOTA + TOPK]
        eps = cst[:, C_EPS:C_EPS + 1]

        def table(at, n):
            t = cst[:, at:at + 2 * TT * n].rearrange("p (k t n) -> p k t n", k=2, t=TT)
            return t[:, 0], t[:, 1]

        def xt(c):
            return (xt_hi[:, c, :], xt_lo[:, c, :]) if c < KC else (xt2_hi[:, c - KC, :], xt2_lo[:, c - KC, :])

        def spread(ap, shape, axis):
            return ap.unsqueeze(axis).to_broadcast(shape)

        NH0 = 16
        HD0 = NH0
        QK_AT = {"moba": 0, "ret": MOBA_H, "mla": MOBA_H + RET_H}
        PR_AT = {"moba": 0, "mla": MOBA_H}

        block = ctx.enter_context(nc.Block())

        @block.sync
        def _(sp):
            def load(u, src, at=0):
                if u >= RING:
                    sp.wait_ge(lo_ready, 2 * (u - RING + 1) + at * 2)
                sp.dma_start(raw[:, u % RING, :], src).then_inc(raw_in[u % RING], 16)

            def segment(name, first=0):
                u0, n = SEG[name]
                u = u0 + first
                if first == 0 and u0 == 0:
                    for k in range(RING):
                        load(k, w[name][k])
                    u = RING
                whole = (u0 + n - u) // RING * RING
                if whole > RING:
                    with sp.Fori(0, whole // RING) as i:
                        for k in range(RING):
                            load(u + k, w[name][i * RING + (u - u0 + k)], i * RING)
                    u += whole
                while u < u0 + n:
                    load(u, w[name][u - u0])
                    u += 1

            sp.dma_start(h[:], x).then_inc(s_cst, 16)
            sp.dma_start(cst[:], consts).then_inc(s_cst, 16)
            sp.dma_start(gain[:], gains).then_inc(s_cst, 16)
            sp.dma_start(dec[:], decay).then_inc(s_dec, 16)
            sp.dma_start(gnb[:], gn_gain.partition_broadcast(P)).then_inc(s_dec, 16)
            segment("in")
            segment("eo")
            for layer in range(2):
                segment(f"q{layer}")
                sp.wait_ge(half_used, 2 * SEG[f"q{layer}"][0])
                sp.dma_start(kys[:], peer_keys[layer]).then_inc(s_keys, 16)
                segment(f"u{layer}")
                segment(f"v{layer}")
                if layer == 0:
                    for name in ("down", "uq", "ukv", "oo"):
                        segment(name)
            sp.wait_ge(half_used, 2 * N_UNITS)
            sp.dma_start(fing[:], fin_gain.partition_broadcast(P)).then_inc(s_fing, 16)
            sp.wait_ge(src_ready, len(TURNS) + 1)
            sp.dma_start(out, fin[:]).then_inc(s_out, 16)
            sp.wait_ge(s_out, 16)

        @block.scalar
        def _(act):
            nxt = [0]
            own = [0]

            def hi(u, at=0):
                act.wait_ge(raw_in[u % RING], 16 * (u // RING + 1) + at * (16 // RING))
                for v in (2 * u, 2 * u + 1):
                    if v >= SPLITS or not isinstance(at, int):
                        act.wait_ge(half_used, max(v - SPLITS + 1, 0) + at * 2)
                    act.activation(w_hi[:, v % SPLITS, :], raw[:, u % RING, v % 2 * HB:(v % 2 + 1) * HB],
                                   ACT.Copy).then_inc(hi_ready, 1)

            def hi_until(u):
                while nxt[0] < min(u, N_UNITS):
                    hi(nxt[0])
                    nxt[0] += 1

            def turn(name):
                at, c0, n, g = TURN_AT[name]
                for c in range(n):
                    act.wait_ge(turn_ps, at + c + 1)
                    scale = 1.0 if g is None else gain[:, g + c:g + c + 1]
                    act.activation(xt(c0 + c)[0], banks[c % 4][:, 0:SEQ], ACT.Copy, scale=scale).then_inc(turn_hi, 1)

            def squares(n_at, srcs, width):
                act.wait_ge(ms_ready, n_at + 1)
                for k, (src, scratch) in enumerate(srcs):
                    act.activation(scratch, src, ACT.Square, accum_out=stat[:, k:k + 1]).then_inc(act_step, 1)
                    own[0] += 1
                act.wait_ge(act_step, own[0])
                for k in range(len(srcs)):
                    ins = act.activation(stat[:, 4 + k:5 + k], stat[:, k:k + 1], ACT.Sqrt, bias=eps, scale=1.0 / width[k])
                    if k < len(srcs) - 1:
                        own[0] += 1
                        ins.then_inc(act_step, 1)
                    else:
                        ins.then_inc(sq_ready, 1)
                act.wait_ge(act_step, own[0])

            def block_out(n, dests):
                act.wait_ge(half_used, 2 * n)
                for k, (dst, src) in enumerate(dests):
                    ins = act.activation(dst, src, ACT.Copy)
                ins.then_inc(blk_act, 1)

            def heads_out(at, n, dst):
                for k in range(0, n, 2):
                    act.wait_ge(hd_ps, at + k + 1)
                    act.activation(dst(k), trn[k % 2][0:dst(k).shape[0], 0:SEQ], ACT.Copy).then_inc(hd_act, 1)

            def softmax(name, heads, sc, pr, row, scale):
                at = PR_AT[name]
                for n in range(heads):
                    act.wait_ge(masked, QK_AT[name] + n + 1)
                    if at + n >= 2:
                        act.wait_ge(pt_ps, at + n - 1)
                    act.activation(pr[:, n % 2, 0:P], sc[:, n % 2, 0:P], ACT.Exp, bias=row[:, 1, 0, n:n + 1],
                                   scale=scale, accum_out=row[:, 2, 0, n:n + 1])
                    act.activation(pr[:, n % 2, P:3 * P], sc[:, n % 2, P:3 * P], ACT.Exp, bias=row[:, 1, 1, n:n + 1],
                                   scale=scale, accum_out=row[:, 2, 1, n:n + 1]).then_inc(probs, 1)

            def peer(layer):
                u0, n = SEG[f"q{layer}"]
                for k in range(n):
                    hi_until(u0 + k + 2)
                    act.wait_ge(half_used, 2 * (u0 + k + 1))
                    act.activation(qry_t[:, k, :], sco[k % 2][:, 0:SEQ], ACT.Copy).then_inc(a_read, 1)
                u0, n = SEG[f"u{layer}"]
                for half in range(2):
                    if half:
                        act.wait_ge(listed, layer + 1)
                    else:
                        act.wait_ge(s_rd, (layer + 1) * (LISTS // 4))
                    at = half * (n // 2)
                    with act.Fori(0, n // 2 // RING) as i:
                        for k in range(RING):
                            hi(u0 + at + k + 1, i * RING)
                            act.wait_ge(half_used, i * (2 * RING) + 2 * (u0 + at + k + 1))
                            act.activation(a_t[:, i * RING + (at + k), :], sco[k % 2][:, 0:SEQ],
                                           ACT.Gelu).then_inc(a_read, 1)
                nxt[0] += n
                act.wait_ge(shifted, layer + 1)
                act.activation(tops[:], tops[:], ACT.Exp).then_inc(expd, 1)
                act.wait_ge(pk_rd, 3 * (layer + 1))
                with act.Fori(0, SEQ // 4 // HOTS) as i:
                    for k in range(HOTS):
                        act.wait_ge(hot_ready, i * HOTS + (layer * (SEQ // 4) + k + 1))
                        for m in range(4):
                            ins = act.activation(hot1[:, k, m, :], hot1[:, k, m, :], ACT.Copy,
                                                 scale=pick_t[:, 2, bass.ds(i * (4 * HOTS) + (4 * k + m), 1)])
                        ins.then_inc(hot_gated, 1)
                u0, n = SEG[f"v{layer}"]
                act.wait_ge(g_rd, (layer + 1) * (SEQ // 4))
                with act.Fori(0, n // RING - 1) as i:
                    for k in range(RING):
                        gate_tile(layer, i * RING, k)
                        hi(u0 + k + 1, i * RING)
                nxt[0] += n - RING
                for k in range(n - RING, n):
                    gate_tile(layer, 0, k)
                    hi_until(u0 + k + 2)

            def gate_tile(layer, i, k):
                act.wait_ge(half_used, i * 2 + 2 * (SEG[f"v{layer}"][0] + k - 1))
                act.activation(ga_hi[:, k % 2, :], a_t[:, i + k, :], ACT.Copy).then_inc(ga_hi_ready, 1)

            act.wait_ge(s_cst, 48)
            squares(0, [(h[:, t, :], xn0[:, t, :]) for t in range(TT)], [D] * TT)
            hi_until(1)
            turn("attn0")
            with act.Fori(0, IN_FULL) as i:
                for k in range(KC):
                    hi(k + 1, i * KC)
                act.wait_ge(half_used, i * (2 * KC) + 2 * KC)
                for half in range(2):
                    ins = act.activation(proj[:, 0, bass.ds(i * UW + half * HB, HB)], acc[half][:, :], ACT.Copy)
                ins.then_inc(blk_act, 1)
            nxt[0] += IN_FULL * KC
            end = SEG["eo"][0]
            hi_until(end + 1)
            block_out(end, [(proj[:, 0, IN_FULL * UW:], acc[0][:, :])])
            heads_out(0, NH0, lambda k: qk_t[:, k, :])
            act.wait_ge(blk_act, IN_FULL + 1)
            act.wait_ge(blk_dve, IN_FULL + 1)
            for t in range(TT):
                ins = act.activation(proj[:, t, COL_RG:], proj[:, t, COL_RG:], ACT.Silu)
            ins.then_inc(swish, 1)
            softmax("moba", MOBA_H, sc0, pr0, row0, MOBA_D ** -0.5)
            act.wait_ge(cen_ready, 1)
            act.activation(tmp0[:].rearrange("p k n -> p (k n)")[:, 0:TT * RET_V_W],
                           xn0[:].rearrange("p t n -> p (t n)"), ACT.Square).then_inc(var_ready, 1)
            act.wait_ge(vsum_ready, 1)
            act.activation(gns[:, 2], gns[:, 1], ACT.Sqrt, bias=eps, scale=1.0 / RET_DV).then_inc(var_ready, 1)
            turn("cat")
            hi_until(SEG["q0"][0] + 1)
            squares(1, [(h[:, t, :], xn0[:, t, :]) for t in range(TT)], [D] * TT)
            turn("ffn0")
            peer(0)
            squares(2, [(h[:, t, :], xn1[:, t, :]) for t in range(TT)], [D] * TT)
            turn("attn1")
            end = SEG["uq"][0]
            hi_until(end + 1)
            block_out(end, [(down[:, 0, k * (MLA_DOWN // 2):(k + 1) * (MLA_DOWN // 2)], acc[k][:, 0:MLA_DOWN // 2])
                            for k in range(2)])
            squares(3, [(down[:, t, a:a + n], xn1[:, t, a:a + n]) for a, n in ((0, Q_RANK), (Q_RANK, KV_RANK))
                        for t in range(TT)], [Q_RANK] * TT + [KV_RANK] * TT)
            turn("down")
            col = 0
            for seg, dst in (("uq", q1), ("ukv", kv)):
                col = 0
                for units, halves in blocks_of(seg):
                    end = units[-1][0] + 1
                    hi_until(end + 1)
                    block_out(end, [(dst[:, 0, col + k * HB:col + (k + 1) * HB], acc[k][:, :]) for k in range(len(halves))])
                    col += len(halves) * HB
            heads_out(HD0, 2 * MLA_H, lambda k: q_t[:, k, :] if k < MLA_H else k_t[:, k - MLA_H, :])
            softmax("mla", MLA_H, sc1, pr1, row1, MLA_QD ** -0.5)
            turn("heads")
            hi_until(SEG["q1"][0] + 1)
            squares(4, [(h[:, t, :], xn1[:, t, :]) for t in range(TT)], [D] * TT)
            turn("ffn1")
            peer(1)
            squares(5, [(h[:, t, :], fin[:, t, :]) for t in range(TT)], [D] * TT)

        @block.vector
        def _(dve):
            nxt = [0]
            own = [0]
            count = {}

            def tick(ins):
                ins.then_inc(dve_step, 1)
                own[0] += 1

            def settle(at=0):
                dve.wait_ge(dve_step, own[0] + at)

            def then(ins, at=0):
                tick(ins)
                settle(at)

            def lo_half(v, at=0):
                dve.wait_ge(hi_ready, v + 1 + at * 2)
                dve.tensor_tensor(w_lo[:, v % SPLITS, :], raw[:, v // 2 % RING, v % 2 * HB:(v % 2 + 1) * HB],
                                  w_hi[:, v % SPLITS, :].bitcast(F32), ALU.subtract).then_inc(lo_ready, 1)

            def lo(u, at=0):
                lo_half(2 * u, at)
                lo_half(2 * u + 1, at)

            def lo_until(u):
                while nxt[0] < min(u, N_UNITS):
                    lo(nxt[0])
                    nxt[0] += 1

            def turn(name):
                at, c0, n, g = TURN_AT[name]
                for c in range(n):
                    dve.wait_ge(turn_hi, at + c + 1)
                    hi_t, lo_t = xt(c0 + c)
                    src = banks[c % 4][:, 0:SEQ]
                    if g is None:
                        ins = dve.tensor_tensor(lo_t, src, hi_t.bitcast(F32), ALU.subtract)
                    else:
                        ins = dve.scalar_tensor_tensor(lo_t, src, gain[:, g + c:g + c + 1], hi_t.bitcast(F32),
                                                       ALU.mult, ALU.subtract)
                    ins.then_inc(turn_lo, 1)

            def normed(n_at, rows, name):
                dve.wait_ge(sq_ready, n_at + 1)
                then(dve.reciprocal(stat[:, 0:len(rows)], stat[:, 4:4 + len(rows)]))
                for k, (dst, src) in enumerate(rows):
                    ins = dve.tensor_scalar(dst, src, stat[:, k:k + 1], None, ALU.mult)
                ins.then_inc(src_ready, 1)

            def block_out(n, dests):
                dve.wait_ge(half_used, 2 * n)
                for dst, src in dests:
                    ins = dve.tensor_copy(dst, src)
                ins.then_inc(blk_dve, 1)

            def residual(n, ms):
                dve.wait_ge(half_used, 2 * n)
                for t in range(TT):
                    for half in range(2):
                        hs = h[:, t, half * HB:(half + 1) * HB]
                        ins = dve.tensor_tensor(hs, acc[2 * t + half][:, :], hs, ALU.add)
                ins.then_inc(ms_ready, 1)

            def rope(xv, heads, r2, tab, tmp):
                cos, sin = table(tab, r2)
                sh = [P, TT, heads, r2]
                cb, sb_ = spread(cos, sh, 2), spread(sin, sh, 2)
                x1, x2 = xv[:, :, :, 0:r2], xv[:, :, :, r2:2 * r2]
                t = [tmp[:, k, 0:TT * heads * r2].rearrange("p (t h r) -> p t h r", t=TT, h=heads) for k in range(4)]
                dve.tensor_tensor(t[0], x1, cb, ALU.mult)
                dve.tensor_tensor(t[1], x2, sb_, ALU.mult)
                dve.tensor_tensor(t[2], x2, cb, ALU.mult)
                then(dve.tensor_tensor(t[3], x1, sb_, ALU.mult))
                dve.tensor_tensor(x1, t[0], t[1], ALU.subtract)
                return dve.tensor_tensor(x2, t[2], t[3], ALU.add)

            def heads_out(at, n, dst):
                for k in range(1, n, 2):
                    dve.wait_ge(hd_ps, at + k + 1)
                    dve.tensor_copy(dst(k), trn[k % 2][0:dst(k).shape[0], 0:SEQ]).then_inc(hd_dve, 1)

            def attend(name, heads, sc, pt, row, scale):
                at, pa = QK_AT[name], PR_AT[name]
                mask = cst[:, C_MASK:C_MASK + 3 * P]
                for s in range(heads + 1):
                    if s < heads:
                        dve.wait_ge(qk_ps, at + s + 1)
                        if pa + s >= 2:
                            dve.wait_ge(probs, pa + s - 1)
                        for t, (a, b) in enumerate(((0, P), (P, 3 * P))):
                            ins = dve.tensor_tensor_reduce(sc[:, s % 2, a:b], sco[s % 2][:, a:b], mask[:, a:b], 1.0, -3.0e38,
                                                           ALU.add, ALU.max, row[:, 0, t, s:s + 1])
                        then(ins)
                        dve.tensor_scalar(row[:, 1, :, s], row[:, 0, :, s], -scale, None, ALU.mult).then_inc(masked, 1)
                    if s:
                        n = s - 1
                        dve.wait_ge(pt_ps, pa + n + 1)
                        if pa + n >= 2:
                            dve.wait_ge(pv_done, at + n - 1)
                        dve.tensor_copy(pt[:, n % 2, :], trn[n % 2][:, 0:3 * P]).then_inc(pt_ready, 1)

            def outputs(name, heads, row, dst):
                dve.wait_ge(pv_done, QK_AT[name] + heads)
                dve.wait_ge(probs, PR_AT[name] + heads)
                then(dve.reciprocal(row[:, 3], row[:, 2]))
                for t in range(TT):
                    for b in range(heads // 8):
                        ins = dve.tensor_tensor(dst[:, t, b * HB:(b + 1) * HB].rearrange("p (h d) -> p h d", h=8),
                                                acc[2 * t + b][:, :].rearrange("p (h d) -> p h d", h=8),
                                                spread(row[:, 3, t, 8 * b:8 * b + 8], [P, 8, 64], 2), ALU.mult)
                return ins

            def peer(layer):
                u0, n = SEG[f"q{layer}"]
                lo_until(u0 + n + 1)
                for g in range(LISTS // 4):
                    dve.wait_ge(s_ps, layer * (LISTS // 4) + g + 1)
                    k = g // 2 * 8 + g % 2
                    dve.tensor_copy(scores[:, k:k + 7:2, :],
                                    trn[g % 2][:, :].rearrange("p (a n) -> p a n", a=4)).then_inc(s_rd, 1)
                dve.wait_ge(s_rd, (layer + 1) * (LISTS // 4))
                u0, n = SEG[f"u{layer}"]
                GROUPS = 2 * RING
                with dve.Fori(0, n // 2 // RING) as i:
                    for g in range(GROUPS):
                        dve.wait_ge(dve_step, i * GROUPS + (own[0] + g))
                        lo_half(2 * (u0 + 1) + g, i * RING)
                        both = [(lst[:, j, :], v16[:, j, :], n16[:, j, :]) for j in range(2)]
                        if g == 0:
                            ins = dve.tensor_copy(lst[:], scores[:, bass.ds(i * 2, 2), :])
                        elif g == 1:
                            for values, top, _ in both:
                                ins = dve.max(top[:, 0:8], values)
                        elif g == 2:
                            for values, top, at in both:
                                dve.max_index(at[:, 0:8], top[:, 0:8], values)
                                ins = dve.match_replace(values, top[:, 0:8], values, LOWEST)
                        elif g == 3:
                            for values, top, _ in both:
                                ins = dve.max(top[:, 8:16], values)
                        elif g == 4:
                            for values, top, at in both:
                                ins = dve.max_index(at[:, 8:16], top[:, 8:16], values)
                        elif g == 5:
                            dve.tensor_copy(best[:, bass.ds(i * 2, 2), :], v16[:])
                            ins = dve.tensor_copy(best_i[:, bass.ds(i * 2, 2), :], n16[:])
                        else:
                            ins = dve.memset(junk[:, g - 6:g - 5], 0.0)
                        ins.then_inc(dve_step, 1)
                own[0] += GROUPS * (n // 2 // RING)
                dve.wait_ge(dve_step, own[0])
                dve.drain().then_inc(listed, 1)
                sh = [P, TOPK, TOPK]
                sums = cand[:].rearrange("p a b -> p (a b)")
                top, at = v16[:, 0, :], n16[:, 0, :]
                STEPS = GROUPS + 2
                with dve.Fori(0, n // 2 // RING) as i:
                    step = 0
                    for g in range(GROUPS):
                        dve.wait_ge(dve_step, i * STEPS + (own[0] + step))
                        lo_half(2 * (u0 + n // 2 + 1) + g, i * RING)
                        if g == 0:
                            ins = dve.tensor_tensor(cand[:], spread(best[:, i * 2, :], sh, 2),
                                                    spread(best[:, i * 2 + 1, :], sh, 1), ALU.add)
                        elif g == 1:
                            ins = dve.max(top[:, 0:8], sums)
                        elif g == 2:
                            dve.max_index(at[:, 0:8], top[:, 0:8], sums)
                            ins = dve.match_replace(sums, top[:, 0:8], sums, LOWEST)
                        elif g == 3:
                            ins = dve.max(top[:, 8:16], sums)
                        elif g == 4:
                            ins = dve.max_index(at[:, 8:16], top[:, 8:16], sums)
                        elif g == 5:
                            dve.tensor_copy(tops[:, i, :], top)
                            dve.tensor_scalar(nab[:, 0, :], at, 4, None, ALU.logical_shift_right)
                            ins = dve.tensor_scalar(nab[:, 1, :], at, 15, None, ALU.bitwise_and)
                        elif g == 6:
                            dve.tensor_copy(f16[:], nab[:]).then_inc(dve_step, 1)
                            step += 1
                            dve.wait_ge(dve_step, i * STEPS + (own[0] + step))
                            for q in range(2):
                                ins = dve.tensor_tensor(eqs[:, q], spread(f16[:, q, :], sh, 2), spread(iota16, sh, 1),
                                                        ALU.is_equal)
                        else:
                            for q in range(2):
                                ins = dve.tensor_tensor(eqs[:, q], eqs[:, q], spread(best_i[:, i * 2 + q, :], sh, 1),
                                                        ALU.mult)
                            ins.then_inc(dve_step, 1)
                            step += 1
                            dve.wait_ge(dve_step, i * STEPS + (own[0] + step))
                            for q in range(2):
                                ins = dve.tensor_reduce(picks[:, q, i, :], eqs[:, q], AX_X, ALU.add)
                        ins.then_inc(dve_step, 1)
                        step += 1
                assert step == STEPS
                own[0] += STEPS * (n // 2 // RING)
                dve.wait_ge(dve_step, own[0])
                nxt[0] += n
                then(dve.tensor_copy(gsum[:, 0, :], tops[:, :, 0]))
                dve.tensor_tensor(tops[:], tops[:], spread(gsum[:, 0, :], [P, HEADS, TOPK], 2),
                                  ALU.subtract).then_inc(shifted, 1)
                dve.wait_ge(expd, layer + 1)
                then(dve.tensor_reduce(gsum[:, 0, :], tops[:], AX_X, ALU.add))
                then(dve.reciprocal(gsum[:, 1, :], gsum[:, 0, :]))
                dve.tensor_tensor(picks[:, 2], tops[:], spread(gsum[:, 1, :], [P, HEADS, TOPK], 2),
                                  ALU.mult).then_inc(gated, 1)
                for q in range(3):
                    dve.wait_ge(pk_ps, 3 * layer + q + 1)
                    dve.tensor_copy(pick_t[:, q, :], trn[q % 2][:, 0:SEQ]).then_inc(pk_rd, 1)
                dve.wait_ge(pk_rd, 3 * layer + 3)
                g0 = layer * (SEQ // 4)

                def hots(i, k):
                    sh4 = [P, 4, P]
                    for q, hot in ((1, hot2), (0, hot1)):
                        ins = dve.tensor_tensor(hot[:, k], spread(iota, sh4, 1), spread(pick_t[:, q, bass.ds(i, 4)], sh4, 2),
                                                ALU.is_equal)
                    ins.then_inc(hot_ready, 1)

                def into_a(i, k):
                    at = a_t[:, :, bass.ds(i, 4)].rearrange("p n t -> p t n")
                    dve.tensor_tensor(at, banks[k][:, :].rearrange("p (t n) -> p t n", t=4), at, ALU.mult).then_inc(g_rd, 1)

                for k in range(HOTS):
                    hots(4 * k, k)
                with dve.Fori(0, SEQ // 4 // HOTS - 1) as i:
                    for k in range(HOTS):
                        dve.wait_ge(g_ps, i * HOTS + (g0 + k + 1))
                        into_a(i * (4 * HOTS) + 4 * k, k)
                        hots(i * (4 * HOTS) + 4 * (HOTS + k), k)
                for k in range(HOTS):
                    dve.wait_ge(g_ps, g0 + SEQ // 4 - HOTS + k + 1)
                    into_a(SEQ - 4 * (HOTS - k), k)
                u0, n = SEG[f"v{layer}"]
                dve.wait_ge(g_rd, (layer + 1) * (SEQ // 4))

                def rest(i, k):
                    dve.wait_ge(ga_hi_ready, i + (layer * NKEYS + k + 1))
                    dve.tensor_tensor(ga_lo[:, k % 2, :], a_t[:, i + k, :], ga_hi[:, k % 2, :].bitcast(F32),
                                      ALU.subtract).then_inc(ga_lo_ready, 1)

                with dve.Fori(0, n // RING - 1) as i:
                    for k in range(RING):
                        rest(i * RING, k)
                        lo(u0 + k + 1, i * RING)
                nxt[0] += n - RING
                for k in range(n - RING, n):
                    rest(0, k)
                    lo_until(u0 + k + 2)
                residual(u0 + n, None)

            dve.wait_ge(s_cst, 48)
            dve.tensor_copy(stat[:, 0:1], eps).then_inc(ms_ready, 1)
            normed(0, [(xn0[:, t, :], h[:, t, :]) for t in range(TT)], "attn0")
            lo_until(1)
            turn("attn0")
            with dve.Fori(0, IN_FULL) as i:
                for k in range(KC):
                    lo(k + 1, i * KC)
                dve.wait_ge(half_used, i * (2 * KC) + 2 * KC)
                for half in range(2):
                    ins = dve.tensor_copy(proj[:, 1, bass.ds(i * UW + half * HB, HB)], acc[2 + half][:, :])
                ins.then_inc(blk_dve, 1)
            nxt[0] += IN_FULL * KC
            end = SEG["eo"][0]
            lo_until(end + 1)
            block_out(end, [(proj[:, 1, IN_FULL * UW:], acc[2][:, :])])
            dve.wait_ge(blk_act, IN_FULL + 1)
            dve.wait_ge(blk_dve, IN_FULL + 1)
            view = proj[:, :, 0:COL_MV].rearrange("p t (h d) -> p t h d", d=MOBA_D)
            rope(view, 2 * MOBA_H, MOBA_ROT // 2, C_MROPE, tmp0[:]).then_inc(roped, 1)
            dve.wait_ge(roped, 1)
            view = proj[:, :, COL_RQ:COL_RV].rearrange("p t (h d) -> p t h d", d=RET_DK)
            rope(view, 2 * RET_H, RET_DK // 2, C_RROPE, tmp0[:]).then_inc(roped, 1)
            heads_out(0, NH0, lambda k: qk_t[:, k, :])
            attend("moba", MOBA_H, sc0, pt0, row0, MOBA_D ** -0.5)
            outputs("moba", MOBA_H, row0, cat).then_inc(o_read, 1)
            dve.wait_ge(s_dec, 32)
            for n in range(RET_H):
                dve.wait_ge(qk_ps, QK_AT["ret"] + n + 1)
                if n >= 2:
                    dve.wait_ge(pv_done, QK_AT["ret"] + n - 1)
                dve.tensor_tensor(sc0[:, n % 2, 0:SEQ], sco[n % 2][:, 0:SEQ], dec[:, n, :], ALU.mult)
                dve.tensor_tensor(sc0[:, n % 2, SEQ:SEQ + P], sco[n % 2][:, SEQ:SEQ + P], dec[:, n, 0:P],
                                  ALU.mult).then_inc(masked, 1)
            dve.wait_ge(pv_done, QK_AT["ret"] + RET_H)
            for b in range(4):
                ins = dve.tensor_reduce(gns[:, 0, b // 2, 4 * (b % 2):4 * (b % 2) + 4],
                                        acc[b][:, :].rearrange("p (h d) -> p h d", h=4), AX_X, ALU.add)
            then(ins)
            then(dve.tensor_scalar(gns[:, 0], gns[:, 0], 1.0 / RET_DV, None, ALU.mult))
            for b in range(4):
                ins = dve.tensor_tensor(xn0[:, b // 2, HB * (b % 2):HB * (b % 2 + 1)].rearrange("p (h d) -> p h d", h=4),
                                        acc[b][:, :].rearrange("p (h d) -> p h d", h=4),
                                        spread(gns[:, 0, b // 2, 4 * (b % 2):4 * (b % 2) + 4], [P, 4, RET_DV], 2),
                                        ALU.subtract)
            ins.then_inc(cen_ready, 1)
            dve.wait_ge(var_ready, 1)
            dve.tensor_reduce(gns[:, 1], tmp0[:].rearrange("p k n -> p (k n)")[:, 0:TT * RET_V_W].rearrange(
                "p (t h d) -> p t h d", t=TT, h=RET_H), AX_X, ALU.add).then_inc(vsum_ready, 1)
            dve.wait_ge(swish, 1)
            for t in range(TT):
                ins = dve.tensor_tensor(proj[:, t, COL_RG:], proj[:, t, COL_RG:], gnb[:], ALU.mult)
            tick(ins)
            dve.wait_ge(var_ready, 2)
            then(dve.reciprocal(gns[:, 3], gns[:, 2]))
            for t in range(TT):
                ins = dve.tensor_tensor(xn0[:, t, :].rearrange("p (h d) -> p h d", h=RET_H),
                                        xn0[:, t, :].rearrange("p (h d) -> p h d", h=RET_H),
                                        spread(gns[:, 3, t, :], [P, RET_H, RET_DV], 2), ALU.mult)
            then(ins)
            for t in range(TT):
                ins = dve.tensor_tensor(cat[:, t, MOBA_W:], xn0[:, t, :], proj[:, t, COL_RG:], ALU.mult)
            ins.then_inc(src_ready, 1)
            turn("cat")
            lo_until(SEG["q0"][0] + 1)
            residual(SEG["q0"][0], None)
            normed(1, [(xn0[:, t, :], h[:, t, :]) for t in range(TT)], "ffn0")
            turn("ffn0")
            peer(0)

            normed(2, [(xn1[:, t, :], h[:, t, :]) for t in range(TT)], "attn1")
            turn("attn1")
            end = SEG["uq"][0]
            lo_until(end + 1)
            block_out(end, [(down[:, 1, k * (MLA_DOWN // 2):(k + 1) * (MLA_DOWN // 2)], acc[2 + k][:, 0:MLA_DOWN // 2])
                            for k in range(2)])
            dve.wait_ge(blk_act, IN_FULL + 2)
            dve.wait_ge(blk_dve, IN_FULL + 2)
            dve.tensor_copy(stat[:, 0:1], eps).then_inc(ms_ready, 1)
            view = down[:, :, Q_RANK + KV_RANK:].rearrange("p t (h d) -> p t h d", h=1)
            then(rope(view, 1, MLA_ROPE // 2, C_LROPE, tmp1[:]))
            ranges = [(t, a, n) for a, n in ((0, Q_RANK), (Q_RANK, KV_RANK)) for t in range(TT)]
            normed(3, [(xn1[:, t, a:a + n], down[:, t, a:a + n]) for t, a, n in ranges], "down")
            for t in range(TT):
                tick(dve.tensor_copy(kf[:, t, :].rearrange("p (h d) -> p h d", h=MLA_H)[:, :, MLA_NOPE:],
                                     spread(down[:, t, Q_RANK + KV_RANK:], [P, MLA_H, MLA_ROPE], 1)))
            turn("down")
            for seg, dst in (("uq", q1), ("ukv", kv)):
                col = 0
                for units, halves in blocks_of(seg):
                    end = units[-1][0] + 1
                    lo_until(end + 1)
                    block_out(end, [(dst[:, 1, col + k * HB:col + (k + 1) * HB], acc[2 + k][:, :])
                                    for k in range(len(halves))])
                    col += len(halves) * HB
            dve.wait_ge(blk_act, IN_FULL + 6)
            dve.wait_ge(blk_dve, IN_FULL + 6)
            view = q1[:].rearrange("p t (h d) -> p t h d", h=MLA_H)[:, :, :, MLA_NOPE:]
            rope(view, MLA_H, MLA_ROPE // 2, C_LROPE, tmp1[:]).then_inc(roped, 1)
            for t in range(TT):
                ins = dve.tensor_copy(kf[:, t, :].rearrange("p (h d) -> p h d", h=MLA_H)[:, :, 0:MLA_NOPE],
                                      kv[:, t, :].rearrange("p (h d) -> p h d", h=MLA_H)[:, :, 0:MLA_NOPE])
            ins.then_inc(roped, 1)
            heads_out(HD0, 2 * MLA_H, lambda k: q_t[:, k, :] if k < MLA_H else k_t[:, k - MLA_H, :])
            attend("mla", MLA_H, sc1, pt1, row1, MLA_QD ** -0.5)
            outputs("mla", MLA_H, row1, o1).then_inc(src_ready, 1)
            turn("heads")
            lo_until(SEG["q1"][0] + 1)
            residual(SEG["q1"][0], None)
            normed(4, [(xn1[:, t, :], h[:, t, :]) for t in range(TT)], "ffn1")
            turn("ffn1")
            peer(1)

            dve.wait_ge(sq_ready, 6)
            then(dve.reciprocal(stat[:, 0:TT], stat[:, 4:4 + TT]))
            dve.wait_ge(s_fing, 16)
            for t in range(TT):
                ins = dve.scalar_tensor_tensor(fin[:, t, :], h[:, t, :], stat[:, t:t + 1], fing[:], ALU.mult, ALU.mult)
            ins.then_inc(src_ready, 1)

        @block.tensor
        def _(pe):
            def split(v, at=0):
                pe.wait_ge(lo_ready, v + 1 + at * 2)
                return w_hi[:, v % SPLITS, :], w_lo[:, v % SPLITS, :]

            def unit(u, parts, halves, start, stop, at=0):
                work = [(v, c, half) for v, (c, half) in enumerate(
                    [(parts[0][0], 0), (parts[0][0], 1)] if len(parts) == 1 else [(c, 0) for c, _ in parts])]
                for v, c, half in work:
                    w_h, w_l = split(2 * u + v, at)
                    width = halves[half]
                    xh, xl = xt(c)
                    first, last = start and (v == 0 or half == 1), stop and (v == 1 or len(parts) == 1)
                    for t in range(TT):
                        dst = acc[2 * t + half][:, 0:width]
                        th, tl = xh[:, t * P:(t + 1) * P], xl[:, t * P:(t + 1) * P]
                        pe.matmul(dst, th, w_h[:, 0:width], start=first, stop=False)
                        pe.matmul(dst, tl, w_h[:, 0:width], start=False, stop=False)
                        ins = pe.matmul(dst, th, w_l[:, 0:width], start=False, stop=last)
                    ins.then_inc(half_used, 1)

            blocks = [0]

            def project(seg):
                for units, halves in blocks_of(seg):
                    if blocks[0]:
                        pe.wait_ge(blk_act, blocks[0])
                        pe.wait_ge(blk_dve, blocks[0])
                    for n, (u, parts) in enumerate(units):
                        unit(u, parts, halves, n == 0, n == len(units) - 1)
                    blocks[0] += 1

            def turn(name, src):
                at, _, n, _ = TURN_AT[name]
                pe.wait_ge(src_ready, TURN_NO[name] + 1)
                for c in range(n):
                    if c >= 4:
                        pe.wait_ge(turn_lo, at + c - 3)
                    for t in range(TT):
                        ins = pe.transpose(banks[c % 4][:, t * P:(t + 1) * P], src[:, t, c * P:(c + 1) * P], ident)
                    ins.then_inc(turn_ps, 1)
                pe.wait_ge(turn_lo, at + n)

            def turn_heads(at, n, src, width):
                for k in range(n):
                    if at + k >= 2:
                        pe.wait_ge(hd_dve if k % 2 else hd_act, (at + k) // 2)
                    for t in range(TT):
                        ins = pe.transpose(trn[k % 2][0:width, t * P:(t + 1) * P], src(k, t), ident)
                    ins.then_inc(hd_ps, 1)
                pe.wait_ge(hd_act, (at + n) // 2)
                pe.wait_ge(hd_dve, (at + n) // 2)

            def attend(name, heads, q, k, v, pr, pt):
                at, pa = QK_AT[name], PR_AT[name]
                for s in range(heads + 2):
                    if s < heads:
                        if at + s >= 2:
                            pe.wait_ge(masked, at + s - 1)
                        pe.matmul(sco[s % 2][:, 0:P], q(s)[:, 0:P], k(s)[:, 0:P], start=True, stop=True)
                        pe.matmul(sco[s % 2][:, P:3 * P], q(s)[:, P:SEQ], k(s), start=True, stop=True).then_inc(qk_ps, 1)
                    if 1 <= s <= heads:
                        n = s - 1
                        pe.wait_ge(probs, pa + n + 1)
                        if pa + n >= 2:
                            pe.wait_ge(pt_ready, pa + n - 1)
                        for b in range(3):
                            ins = pe.transpose(trn[n % 2][:, b * P:(b + 1) * P], pr[:, n % 2, b * P:(b + 1) * P], ident)
                        ins.then_inc(pt_ps, 1)
                    if s >= 2:
                        n = s - 2
                        pe.wait_ge(pt_ready, pa + n + 1)
                        cols = slice((n % 8) * 64, (n % 8) * 64 + 64)
                        o0, o1_ = acc[n // 8][:, cols], acc[2 + n // 8][:, cols]
                        pe.matmul(o0, pt[:, n % 2, 0:P], v(n, 0), start=True, stop=True)
                        pe.matmul(o1_, pt[:, n % 2, P:2 * P], v(n, 0), start=True, stop=False)
                        pe.matmul(o1_, pt[:, n % 2, 2 * P:], v(n, 1), start=False, stop=True).then_inc(pv_done, 1)

            def turned_unit(u, bank, at=0):
                dst = sco[bank][:, 0:SEQ]
                for c in range(KC):
                    if c % 4 == 0:
                        w_h, w_l = split(2 * u + c // 4, at)
                    wh, wl = w_h[:, c % 4 * P:(c % 4 + 1) * P], w_l[:, c % 4 * P:(c % 4 + 1) * P]
                    xh, xl = xt(c)
                    pe.matmul(dst, wh, xh, start=(c == 0), stop=False)
                    pe.matmul(dst, wl, xh, start=False, stop=False)
                    ins = pe.matmul(dst, wh, xl, start=False, stop=(c == KC - 1))
                    if c % 4 == 3:
                        ins.then_inc(half_used, 1)

            def peer(layer):
                b = layer * (PEER_H + NKEYS)
                u0, n = SEG[f"q{layer}"]
                for k in range(n):
                    if b + k >= 2:
                        pe.wait_ge(a_read, b + k - 1)
                    turned_unit(u0 + k, k % 2)
                b += n
                pe.wait_ge(s_keys, 16 * (layer + 1))
                pe.wait_ge(a_read, b)
                g0 = layer * (LISTS // 4)
                for g in range(LISTS // 4):
                    if g >= 2:
                        pe.wait_ge(s_rd, g0 + g - 1)
                    for m in range(4):
                        t, hh, half = g // 4, g // 2 % 2 * 4 + m, g % 2
                        rows = slice(64 * half, 64 * half + 64)
                        ins = pe.matmul(trn[g % 2][:, m * P:(m + 1) * P], qry_t[rows, hh, t * P:(t + 1) * P],
                                        kys[rows, hh, :], start=True, stop=True)
                    ins.then_inc(s_ps, 1)
                u0, n = SEG[f"u{layer}"]
                with pe.Fori(0, n // (2 * RING)) as i:
                    for k in range(2 * RING):
                        pe.wait_ge(a_read, i * (2 * RING) + (b + k - 1))
                        turned_unit(u0 + k, k % 2, i * (2 * RING))
                pe.wait_ge(gated, layer + 1)
                for q in range(3):
                    if q == 2:
                        pe.wait_ge(pk_rd, 3 * layer + 1)
                    for t in range(TT):
                        ins = pe.transpose(trn[q % 2][:, t * P:(t + 1) * P],
                                           picks[:, q, t * PEER_H:(t + 1) * PEER_H, :].rearrange("p h k -> p (h k)"), ident)
                    ins.then_inc(pk_ps, 1)
                g0 = layer * (SEQ // 4)

                def gates(i, k, slot):
                    pe.wait_ge(hot_gated, i + (g0 + k + 1))
                    for m in range(4):
                        ins = pe.matmul(banks[slot][:, m * P:(m + 1) * P], hot2[:, slot, m, :].bitcast(F32), hot1[:, slot, m, :],
                                        start=True, stop=True)
                    ins.then_inc(g_ps, 1)

                pe.wait_ge(pk_rd, 3 * layer + 3)
                for k in range(HOTS):
                    gates(0, k, k)
                with pe.Fori(0, SEQ // 4 // HOTS - 1) as i:
                    for k in range(HOTS):
                        pe.wait_ge(g_rd, i * HOTS + (g0 + k + 1))
                        gates(i * HOTS, HOTS + k, k)
                u0, n = SEG[f"v{layer}"]

                def expert_unit(i, k, start, stop):
                    pe.wait_ge(ga_lo_ready, i + (layer * NKEYS + k + 1))
                    for half in range(2):
                        w_h, w_l = split(2 * (u0 + k) + half, i)
                        for t in range(TT):
                            dst = acc[2 * t + half][:, :]
                            ah, al = ga_hi[:, k % 2, t * P:(t + 1) * P], ga_lo[:, k % 2, t * P:(t + 1) * P]
                            pe.matmul(dst, ah, w_h, start=start, stop=False, skip_group_check=True)
                            pe.matmul(dst, al, w_h, start=False, stop=False, skip_group_check=True)
                            ins = pe.matmul(dst, ah, w_l, start=False, stop=stop, skip_group_check=True)
                        ins.then_inc(half_used, 1)

                for k in range(RING):
                    expert_unit(0, k, k == 0, False)
                with pe.Fori(0, n // RING - 2) as i:
                    for k in range(RING):
                        expert_unit(i * RING, RING + k, False, False)
                for k in range(n - RING, n):
                    expert_unit(0, k, False, k == n - 1)

            pe.wait_ge(s_cst, 48)
            turn("attn0", xn0)
            for k in range(KC):
                unit(k, [(k, 0)], [HB, HB], k == 0, k == KC - 1)
            with pe.Fori(1, IN_FULL) as i:
                pe.wait_ge(blk_act, i)
                pe.wait_ge(blk_dve, i)
                for k in range(KC):
                    unit(k, [(k, 0)], [HB, HB], k == 0, k == KC - 1, i * KC)
            blocks[0] = IN_FULL
            project("in")
            pe.wait_ge(roped, 2)
            pe.wait_ge(blk_act, blocks[0])
            pe.wait_ge(blk_dve, blocks[0])
            cols = [0, MOBA_W, COL_RQ, COL_RQ + RET_QK_W]
            turn_heads(0, NH0, lambda k, t: proj[:, t, cols[k // 4] + (k % 4) * P:cols[k // 4] + (k % 4 + 1) * P], P)

            def pair(base):
                return lambda n: qk_t[64 * (n % 2):64 * (n % 2) + 64, base + n // 2, :]

            attend("moba", MOBA_H, pair(0), pair(4), lambda n, t: proj[:, t, COL_MV + n * 64:COL_MV + (n + 1) * 64], pr0, pt0)
            pe.wait_ge(o_read, 1)
            at = QK_AT["ret"]
            for s in range(RET_H + 1):
                if s < RET_H:
                    pe.wait_ge(masked, at + s - 1)
                    q, k = pair(8)(s), pair(12)(s)
                    pe.matmul(sco[s % 2][:, 0:SEQ], k[:, 0:P], q, start=True, stop=True)
                    pe.matmul(sco[s % 2][:, SEQ:SEQ + P], k[:, P:SEQ], q[:, P:SEQ], start=True, stop=True).then_inc(qk_ps, 1)
                if s:
                    n = s - 1
                    pe.wait_ge(masked, at + n + 1)
                    c = slice((n % 4) * RET_DV, (n % 4 + 1) * RET_DV)
                    v = [proj[:, t, COL_RV + n * RET_DV:COL_RV + (n + 1) * RET_DV] for t in range(TT)]
                    pe.matmul(acc[n // 4][:, c], sc0[:, n % 2, 0:P], v[0], start=True, stop=True)
                    pe.matmul(acc[2 + n // 4][:, c], sc0[:, n % 2, P:SEQ], v[0], start=True, stop=False)
                    pe.matmul(acc[2 + n // 4][:, c], sc0[:, n % 2, SEQ:SEQ + P], v[1], start=False,
                              stop=True).then_inc(pv_done, 1)
            turn("cat", cat)
            blocks[0] = 0
            project("eo")
            turn("ffn0", xn0)
            peer(0)
            turn("attn1", xn1)
            blocks[0] = 0
            project("down")
            blocks[0] = IN_FULL + 2
            turn("down", xn1)
            project("uq")
            project("ukv")
            pe.wait_ge(roped, 4)
            pe.wait_ge(blk_act, blocks[0])
            pe.wait_ge(blk_dve, blocks[0])
            turn_heads(HD0, 2 * MLA_H, lambda k, t: (q1 if k < MLA_H else kf)[:, t, (k % MLA_H) * MLA_QD:(k % MLA_H + 1) * MLA_QD],
                       MLA_QD)
            attend("mla", MLA_H, lambda n: q_t[:, n, :], lambda n: k_t[:, n, :],
                   lambda n, t: kv[:, t, n * 128 + MLA_NOPE:(n + 1) * 128], pr1, pt1)
            turn("heads", o1)
            blocks[0] = 0
            project("oo")
            turn("ffn1", xn1)
            peer(1)


def kernel(**inputs):
    import numpy as _np
    import concourse.bacc as _bacc
    from concourse import mybir as _mybir
    from concourse.bass_utils import run_bass_kernel_spmd as _run

    a = {k: _np.asarray(v) for k, v in inputs.items()}

    def rows(m):
        return m.reshape(-1, P, UW)

    def halves(m):
        return m.reshape(-1, 2, P, HB).transpose(0, 2, 1, 3).reshape(-1, P, UW)

    def turned(m):
        return m.reshape(-1, P, KC, P).transpose(0, 3, 2, 1).reshape(-1, P, UW)

    def column(v):
        return v.reshape(-1, P).T

    w_in = a["ev_w_in"][0]
    full = IN_FULL * UW
    down = _np.zeros((D, 2, HB), _np.float32)
    down[:, :, :MLA_DOWN // 2] = a["od_w_down"][0].reshape(D, 2, MLA_DOWN // 2)
    uq, ukv = a["od_w_uq"][0], a["od_w_ukv"][0]
    arrays = {
        "w_in": _np.concatenate([rows(w_in[:, k * UW:(k + 1) * UW]) for k in range(IN_FULL)] + [halves(w_in[:, full:])]),
        "w_eo": rows(a["ev_w_o"][0]),
        "w_down": rows(down),
        "w_uq": _np.concatenate([rows(uq[:, :UW]), halves(uq[:, UW:])]),
        "w_ukv": _np.concatenate([rows(ukv[:, :UW]), rows(ukv[:, UW:])]),
        "w_oo": rows(a["od_w_o"][0]),
    }
    for layer in range(2):
        arrays[f"w_q{layer}"] = turned(a["peer_wq"][layer].T)
        arrays[f"w_u{layer}"] = turned(a["peer_u"][layer])
        arrays[f"w_v{layer}"] = rows(a["peer_v"][layer])
    arrays["x"] = a["x"].reshape(TT, P, D).transpose(1, 0, 2)
    arrays["keys"] = a["peer_keys"].transpose(0, 2, 4, 1, 3).reshape(2, P, PEER_H, NKEYS)
    arrays["gains"] = _np.concatenate([column(a["attn_norm"][0]), column(a["ffn_norm"][0]), column(a["attn_norm"][1]),
                                       column(a["ffn_norm"][1]), column(a["od_q_norm"][0]), column(a["od_kv_norm"][0])], axis=1)
    arrays["gn_gain"] = a["ev_ret_gn"][0]
    arrays["fin_gain"] = a["final_norm"]
    arrays["consts"] = constants()
    arrays["decay"] = decay_table()
    arrays = {f"in_{k}_dram": _np.ascontiguousarray(v) for k, v in arrays.items()}

    nc = _bacc.Bacc("TRN2", target_bir_lowering=False, num_devices=1)
    t = {k[3:-5]: nc.dram_tensor(k, v.shape, _mybir.dt.from_np(v.dtype), kind="ExternalInput").ap() for k, v in arrays.items()}
    out = nc.dram_tensor("out_dram", (P, TT, D), _mybir.dt.float32, kind="ExternalOutput").ap()
    build(nc, t["x"], {k[2:]: v for k, v in t.items() if k.startswith("w_")}, t["keys"], t["gains"], t["gn_gain"],
          t["fin_gain"], t["consts"], t["decay"], out)
    r = _run(nc, [arrays], core_ids=[0])
    return r.results[0]["out_dram"].transpose(1, 0, 2).reshape(1, SEQ, D)
```

```python
from contextlib import ExitStack

import numpy as np

import concourse.bass as bass
from concourse import mybir

ALU = mybir.AluOpType
ACT = mybir.ActivationFunctionType
AX_X = mybir.AxisListType.X
F32 = mybir.dt.float32
F32R = mybir.dt.float32r
U32 = mybir.dt.uint32

P = 128
SEQ = 256
TT = SEQ // P
D = 1024
KC = D // P
EPS = 1e-6
ROPE_THETA, RET_THETA = 500000.0, 10000.0

MOBA_H, MOBA_D, MOBA_ROT = 8, 64, 16
RET_H, RET_DK, RET_DV = 8, 64, 128
MOBA_W, RET_QK_W, RET_V_W = MOBA_H * MOBA_D, RET_H * RET_DK, RET_H * RET_DV
COL_MV = 2 * MOBA_W
COL_RQ = 3 * MOBA_W
COL_RV = COL_RQ + 2 * RET_QK_W
COL_RG = COL_RV + RET_V_W
EVEN_IN = COL_RG + RET_V_W
EVEN_OUT = MOBA_W + RET_V_W
MLA_H, MLA_NOPE, MLA_ROPE, MLA_V = 16, 64, 32, 64
MLA_QD = MLA_NOPE + MLA_ROPE
Q_RANK, KV_RANK = 512, 256
MLA_DOWN = Q_RANK + KV_RANK + MLA_ROPE
PEER_H, NKEYS, TOPK = 8, 128, 16
LISTS = TT * PEER_H * 2
HEADS = TT * PEER_H

UW = 1024
HB = 512
RING = 4
SPLITS = 4
HOTS = 4
LOWEST = -3.0e38

C_ID = 0
C_EPS = C_ID + P
C_LATER = C_EPS + 1
C_IOTA = C_LATER
C_MASK = C_IOTA + P
C_MROPE = C_MASK + 3 * P
C_RROPE = C_MROPE + 2 * TT * (MOBA_ROT // 2)
C_LROPE = C_RROPE + 2 * TT * (RET_DK // 2)
C_END = C_LROPE + 2 * TT * (MLA_ROPE // 2)

G_ATTN0, G_FFN0, G_ATTN1, G_FFN1 = 0, KC, 2 * KC, 3 * KC
G_Q = 4 * KC
G_KV = G_Q + Q_RANK // P
G_END = G_KV + KV_RANK // P


def rope_table(rot, theta):
    inv = (1.0 / (np.float32(theta) ** (np.arange(0, rot, 2, dtype=np.float32) / np.float32(rot)))).astype(np.float32)
    ang = np.arange(SEQ, dtype=np.float32)[:, None] * inv[None, :]
    cs = np.stack([np.cos(ang), np.sin(ang)]).astype(np.float32)
    return cs.reshape(2, TT, P, rot // 2).transpose(2, 0, 1, 3).reshape(P, -1)


def constants():
    tri = np.where(np.arange(P)[None, :] <= np.arange(P)[:, None], 0.0, -1.0e30)
    c = np.concatenate([np.eye(P), np.full((P, 1), EPS), np.tile(np.arange(P), (P, 1)), tri, np.zeros((P, P)), tri,
                        rope_table(MOBA_ROT, ROPE_THETA), rope_table(RET_DK, RET_THETA),
                        rope_table(MLA_ROPE, ROPE_THETA)], axis=1)
    assert c.shape[1] == C_END
    return c.astype(np.float32)


def decay_table():
    log_g = np.log(1.0 - 2.0 ** (-5.0 - np.arange(RET_H)))
    diff = np.arange(SEQ)[None, :] - np.arange(P)[:, None]
    d = np.where(diff[:, None, :] >= 0, np.exp(log_g[None, :, None] * np.maximum(diff, 0)[:, None, :]), 0.0)
    return (d * RET_DK ** -0.5).astype(np.float32)


IN_FULL = EVEN_IN // UW
SEG = {}
_at = 0
for _name, _n in (("in", IN_FULL * KC + KC // 2), ("eo", EVEN_OUT // P), ("q0", PEER_H), ("u0", NKEYS), ("v0", NKEYS),
                  ("down", KC), ("uq", 6), ("ukv", 4), ("oo", KC), ("q1", PEER_H), ("u1", NKEYS), ("v1", NKEYS)):
    SEG[_name] = (_at, _n)
    _at += _n
N_UNITS = _at

TURNS = (("attn0", 0, KC, G_ATTN0), ("moba", 0, MOBA_W // P, None), ("ret", MOBA_W // P, RET_H, None), ("ffn0", 0, KC, G_FFN0),
         ("attn1", 0, KC, G_ATTN1), ("down", 0, (Q_RANK + KV_RANK) // P, G_Q), ("heads", 0, KC, None),
         ("ffn1", 0, KC, G_FFN1))
TURN_AT = {}
_at = 0
for _name, _c0, _n, _g in TURNS:
    TURN_AT[_name] = (_at, _c0, _n, _g)
    _at += _n
TURN_NO = {t[0]: i + (t[0] == "ffn1") for i, t in enumerate(TURNS)}


def blocks_of(seg):
    u0, _ = SEG[seg]
    if seg == "in":
        first = u0 + IN_FULL * KC
        return [([(first + n, [(2 * n, 0), (2 * n + 1, HB)]) for n in range(KC // 2)], [HB])]
    if seg == "eo":
        return [([(u0 + c, [(c, 0)]) for c in range(EVEN_OUT // P)], [HB, HB])]
    if seg == "down":
        return [([(u0 + c, [(c, 0)]) for c in range(KC)], [MLA_DOWN // 2, MLA_DOWN // 2])]
    if seg == "uq":
        return [([(u0 + c, [(c, 0)]) for c in range(4)], [HB, HB]),
                ([(u0 + 4 + n, [(2 * n, 0), (2 * n + 1, HB)]) for n in range(2)], [HB])]
    if seg == "ukv":
        return [([(u0 + 2 * b + n, [(4 + n, 0)]) for n in range(2)], [HB, HB]) for b in range(2)]
    return [([(u0 + c, [(c, 0)]) for c in range(KC)], [HB, HB])]


def build(nc, x, w, peer_keys, gains, gn_gain, fin_gain, consts, decay, out):
    with ExitStack() as ctx:
        def sb(name, shape, dt=F32, scope=ctx):
            return scope.enter_context(nc.sbuf_tensor(name, shape, dt))

        def sem(name):
            return ctx.enter_context(nc.semaphore(name))

        cst = sb("cst", [P, C_END])
        gain = sb("gain", [P, G_END])
        h = sb("h", [P, TT, D])
        xt_hi = sb("xt_hi", [P, KC, SEQ], F32R)
        xt_lo = sb("xt_lo", [P, KC, SEQ], F32R)
        raw = sb("raw", [P, RING, UW])
        w_hi = sb("w_hi", [P, SPLITS, HB], F32R)
        w_lo = sb("w_lo", [P, SPLITS, HB], F32R)
        stat = sb("stat", [P, 8])
        picks = sb("picks", [P, 3, HEADS, TOPK])
        gsum = sb("gsum", [P, 2, HEADS])
        spare = sb("spare", [P, 16])

        s0 = ExitStack()
        xn0 = sb("xn0", [P, TT, D], F32, s0)
        xt2_hi = sb("xt2_hi", [P, 4, SEQ], F32R, s0)
        xt2_lo = sb("xt2_lo", [P, 4, SEQ], F32R, s0)
        proj = sb("proj", [P, TT, EVEN_IN], F32, s0)
        qk_t = sb("qk_t", [P, 16, SEQ], F32, s0)
        dec = sb("dec", [P, RET_H, SEQ], F32, s0)
        cat = sb("cat", [P, TT, EVEN_OUT], F32, s0)
        sc0 = sb("sc0", [P, 2, 3 * P], F32, s0)
        pr0 = sb("pr0", [P, 2, 3 * P], F32, s0)
        pt0 = sb("pt0", [P, 2, 3 * P], F32, s0)
        row0 = sb("row0", [P, 6, TT, MOBA_H], F32, s0)
        tmp0 = sb("tmp0", [P, 4, TT * 16 * 32], F32, s0)
        gnb = sb("gnb", [P, RET_V_W], F32, s0)
        gns = sb("gns", [P, 4, TT, RET_H], F32, s0)
        s0.close()
        s1 = ExitStack()
        xn1 = sb("xn1", [P, TT, D], F32, s1)
        down = sb("down", [P, TT, MLA_DOWN], F32, s1)
        q1 = sb("q1", [P, TT, MLA_H * MLA_QD], F32, s1)
        v1 = sb("v1", [P, TT, MLA_H * MLA_V], F32, s1)
        kf = sb("kf", [P, TT, MLA_H * MLA_QD], F32, s1)
        q_t = sb("q_t", [MLA_QD, MLA_H, SEQ], F32, s1)
        k_t = sb("k_t", [MLA_QD, MLA_H, SEQ], F32, s1)
        sc1 = sb("sc1", [P, 2, 3 * P], F32, s1)
        pr1 = sb("pr1", [P, 2, 3 * P], F32, s1)
        pt1 = sb("pt1", [P, 2, 3 * P], F32, s1)
        row1 = sb("row1", [P, 6, TT, MLA_H], F32, s1)
        tmp1 = sb("tmp1", [P, 4, TT * MLA_H * 16], F32, s1)
        o1 = sb("o1", [P, TT, D], F32, s1)
        s1.close()
        s2 = ExitStack()
        a_t = sb("a_t", [P, NKEYS, SEQ], F32, s2)
        s3 = ExitStack()
        best = sb("best", [P, LISTS, TOPK], F32, s3)
        best_i = sb("best_i", [P, LISTS, TOPK], F32, s3)
        tops = sb("tops", [P, HEADS, TOPK], F32, s3)
        lst = sb("lst", [P, 2, NKEYS], F32, s3)
        v16 = sb("v16", [P, 2, TOPK], F32, s3)
        n16 = sb("n16", [P, 2, TOPK], U32, s3)
        junk = sb("junk", [P, 4], F32, s3)
        nab = sb("nab", [P, 2, TOPK], U32, s3)
        cand = sb("cand", [P, TOPK, TOPK], F32, s3)
        eqs = sb("eqs", [P, 2, TOPK, TOPK], F32, s3)
        s3.close()
        s4 = ExitStack()
        pick_t = sb("pick_t", [P, 3, SEQ], F32, s4)
        hot2 = xt_lo[:].rearrange("p a b -> p (a b)").rearrange("p (k m n) -> p k m n", k=HOTS, m=4)
        hot1 = sb("hot1", [P, HOTS, 4, P], F32, s4)
        s4.close()
        s5 = ExitStack()
        ga_hi = sb("ga_hi", [P, 2, SEQ], F32R, s5)
        ga_lo = sb("ga_lo", [P, 2, SEQ], F32R, s5)
        fing = sb("fing", [P, D], F32, s5)
        s5.close()
        s2.close()
        s6 = ExitStack()
        fin = sb("fin", [P, TT, D], F32, s6)
        kys = sb("kys", [P, PEER_H, NKEYS], F32, s6)
        qry_t = sb("qry_t", [P, PEER_H, SEQ], F32, s6)
        s6.close()
        S_TILES = LISTS * NKEYS // SEQ
        scores = a_t[:, NKEYS - S_TILES:, :].rearrange("p a (b n) -> p (a b) n", n=NKEYS)

        acc = [ctx.enter_context(nc.psum_tensor(f"acc{i}", [P, HB], F32)) for i in range(4)]
        sco = [ctx.enter_context(nc.psum_tensor(f"sco{i}", [P, HB], F32)) for i in range(2)]
        trn = [ctx.enter_context(nc.psum_tensor(f"trn{i}", [P, HB], F32)) for i in range(2)]

        banks = [trn[0], sco[0], trn[1], sco[1]]

        s_x = [sem(f"s_x{t}") for t in range(TT)]
        s_cst = sem("s_cst")
        s_tab = sem("s_tab")
        s_dec = sem("s_dec")
        s_keys = sem("s_keys")
        s_fing = sem("s_fing")
        s_out = sem("s_out")
        raw_in = [sem(f"raw_in{i}") for i in range(RING)]
        hi_ready = sem("hi_ready")
        lo_ready = sem("lo_ready")
        half_used = sem("half_used")
        act_step = sem("act_step")
        dve_step = sem("dve_step")
        src_ready = sem("src_ready")
        turn_ps = sem("turn_ps")
        turn_hi = sem("turn_hi")
        turn_lo = sem("turn_lo")
        sq_ready = sem("sq_ready")
        ms_ready = sem("ms_ready")
        blk_act = sem("blk_act")
        blk_dve = sem("blk_dve")
        roped = sem("roped")
        hd_ps = sem("hd_ps")
        hd_act = sem("hd_act")
        hd_dve = sem("hd_dve")
        qk_ps = sem("qk_ps")
        masked = sem("masked")
        probs = sem("probs")
        pt_ps = sem("pt_ps")
        pt_ready = sem("pt_ready")
        pv_done = sem("pv_done")
        cen_ready = sem("cen_ready")
        var_ready = sem("var_ready")
        vsum_ready = sem("vsum_ready")
        swish = sem("swish")
        swish_gain = sem("swish_gain")
        a_read = sem("a_read")
        s_ps = sem("s_ps")
        s_rd = sem("s_rd")
        listed = sem("listed")
        shifted = sem("shifted")
        expd = sem("expd")
        gated = sem("gated")
        pk_ps = sem("pk_ps")
        pk_rd = sem("pk_rd")
        hot_ready = sem("hot_ready")
        hot_gated = sem("hot_gated")
        g_ps = sem("g_ps")
        g_rd = sem("g_rd")
        ga_hi_ready = sem("ga_hi_ready")
        ga_lo_ready = sem("ga_lo_ready")

        ident = cst[:, C_ID:C_ID + P]
        iota = cst[:, C_IOTA:C_IOTA + P]
        iota16 = cst[:, C_IOTA:C_IOTA + TOPK]
        eps = cst[:, C_EPS:C_EPS + 1]

        def table(at, n):
            t = cst[:, at:at + 2 * TT * n].rearrange("p (k t n) -> p k t n", k=2, t=TT)
            return t[:, 0], t[:, 1]

        def xt(c):
            return (xt_hi[:, c, :], xt_lo[:, c, :]) if c < KC else (xt2_hi[:, c - KC, :], xt2_lo[:, c - KC, :])

        def spread(ap, shape, axis):
            return ap.unsqueeze(axis).to_broadcast(shape)

        def keys_values_out(copy, t, b, k):
            src = acc[2 * t + k][:, :].rearrange("p (h d) -> p h d", h=4)
            first = 8 * b + 4 * k
            copy(kf[:, t, :].rearrange("p (h d) -> p h d", h=MLA_H)[:, first:first + 4, 0:MLA_NOPE], src[:, :, 0:MLA_NOPE])
            return copy(v1[:, t, first * MLA_V:(first + 4) * MLA_V].rearrange("p (h d) -> p h d", h=4), src[:, :, MLA_NOPE:])

        LATENTS = ((0, Q_RANK), (Q_RANK, KV_RANK))
        NH0 = 16
        IN_BANKS = 2 * IN_FULL + 1
        DOWN_BANKS = IN_BANKS + 2
        UQ_BANKS = DOWN_BANKS + 3
        UKV_BANKS = UQ_BANKS + 4
        QK_AT = {"moba": 0, "ret": MOBA_H, "mla": MOBA_H + RET_H}
        PR_AT = {"moba": 0, "mla": MOBA_H}

        block = ctx.enter_context(nc.Block())

        @block.sync
        def _(sp):
            def load(u, src, at=0):
                if u >= RING:
                    sp.wait_ge(lo_ready, 2 * (u - RING + 1) + at * 2)
                sp.dma_start(raw[:, u % RING, :], src).then_inc(raw_in[u % RING], 16)

            def segment(name, first=0):
                u0, n = SEG[name]
                u = u0 + first
                whole = (u0 + n - u) // RING * RING
                if whole > RING:
                    with sp.Fori(0, whole // RING) as i:
                        for k in range(RING):
                            load(u + k, w[name][i * RING + (u - u0 + k)], i * RING)
                    u += whole
                while u < u0 + n:
                    load(u, w[name][u - u0])
                    u += 1

            sp.dma_start(h[:, 0, :], x[:, 0, :]).then_inc(s_x[0], 16)
            sp.dma_start(cst[:, 0:C_LATER], consts[:, 0:C_LATER]).then_inc(s_cst, 16)
            sp.dma_start(gain[:], gains).then_inc(s_cst, 16)
            sp.dma_start(h[:, 1, :], x[:, 1, :]).then_inc(s_x[1], 16)
            for k in range(RING):
                load(k, w["in"][k])
            sp.dma_start(cst[:, C_LATER:], consts[:, C_LATER:]).then_inc(s_tab, 16)
            sp.dma_start(dec[:], decay).then_inc(s_dec, 16)
            sp.dma_start(gnb[:], gn_gain.partition_broadcast(P)).then_inc(s_dec, 16)
            segment("in", RING)
            segment("eo")
            for layer in range(2):
                segment(f"q{layer}")
                sp.wait_ge(half_used, 2 * SEG[f"q{layer}"][0])
                sp.dma_start(kys[:], peer_keys[layer]).then_inc(s_keys, 16)
                segment(f"u{layer}")
                segment(f"v{layer}")
                if layer == 0:
                    for name in ("down", "uq", "ukv", "oo"):
                        segment(name)
            sp.wait_ge(g_ps, 2 * (SEQ // 4))
            sp.dma_start(fing[:], fin_gain.partition_broadcast(P)).then_inc(s_fing, 16)
            for t in range(TT):
                sp.wait_ge(src_ready, len(TURNS) + 2 + t)
                sp.dma_start(out[:, t, :], fin[:, t, :]).then_inc(s_out, 16)
            sp.wait_ge(s_out, 16 * TT)

        @block.scalar
        def _(act):
            nxt = [0]
            own = [0]

            loads = [0]

            def table_of(func):
                act.activation(spare[:, loads[0]:loads[0] + 1], eps, func)
                loads[0] += 1

            def hi_half(v, at=0):
                u = v // 2
                if v % 2 == 0:
                    act.wait_ge(raw_in[u % RING], 16 * (u // RING + 1) + at * (16 // RING))
                if v >= SPLITS or not isinstance(at, int):
                    act.wait_ge(half_used, max(v - SPLITS + 1, 0) + at * 2)
                act.activation(w_hi[:, v % SPLITS, :], raw[:, u % RING, v % 2 * HB:(v % 2 + 1) * HB],
                               ACT.Copy).then_inc(hi_ready, 1)

            def hi(u, at=0):
                hi_half(2 * u, at)
                hi_half(2 * u + 1, at)

            def hi_until(u):
                while nxt[0] < min(u, N_UNITS):
                    hi(nxt[0])
                    nxt[0] += 1

            def chunk(name, c):
                at, c0, _, g = TURN_AT[name]
                act.wait_ge(turn_ps, at + c + 1)
                scale = 1.0 if g is None else gain[:, g + c:g + c + 1]
                act.activation(xt(c0 + c)[0], banks[c % 4][:, 0:SEQ], ACT.Copy, scale=scale).then_inc(turn_hi, 1)

            def turn(name):
                for c in range(TURN_AT[name][2]):
                    chunk(name, c)

            def turn_project(name, u, n):
                chunk(name, 0)
                chunk(name, 1)
                hi_until(u + 2)
                for k in range(n):
                    if k + 2 < TURN_AT[name][2]:
                        chunk(name, k + 2)
                    hi_until(min(u + k + 3, u + n + 1))

            sums = [0]

            def squares(srcs, widths):
                act.wait_ge(ms_ready, 2 * sums[0] + 1)
                for k, (src, scratch) in enumerate(srcs):
                    act.activation(scratch, src, ACT.Square, accum_out=stat[:, TT * k:TT * k + 1]).then_inc(act_step, 1)
                own[0] += len(srcs)
                sums[0] += 1
                act.wait_ge(act_step, own[0])
                act.wait_ge(ms_ready, 2 * sums[0])
                for k, width in enumerate(widths):
                    ins = act.activation(stat[:, 4 + TT * k:4 + TT * (k + 1)], stat[:, TT * k:TT * (k + 1)], ACT.Sqrt,
                                         bias=eps, scale=1.0 / width)
                ins.then_inc(sq_ready, 1)

            def block_out(n, dests):
                act.wait_ge(half_used, 2 * n)
                for dst, src in dests:
                    act.activation(dst, src, ACT.Copy).then_inc(blk_act, 1)

            def heads_out(at, n, dst):
                for k in range(0, n, 2):
                    act.wait_ge(hd_ps, at + k + 1)
                    act.activation(dst(k), banks[k % 4][0:dst(k).shape[0], 0:SEQ], ACT.Copy).then_inc(hd_act, 1)

            def softmax(name, heads, sc, pr, row, scale, v=None):
                at = PR_AT[name]
                for n in range(heads):
                    act.wait_ge(masked, QK_AT[name] + n + 1)
                    if at + n >= 2:
                        act.wait_ge(pt_ps, at + n - 1)
                    act.activation(pr[:, n % 2, 0:P], sc[:, n % 2, 0:P], ACT.Exp, bias=row[:, 1, 0, n:n + 1],
                                   scale=scale, accum_out=row[:, 2, 0, n:n + 1])
                    act.activation(pr[:, n % 2, P:3 * P], sc[:, n % 2, P:3 * P], ACT.Exp, bias=row[:, 1, 1, n:n + 1],
                                   scale=scale, accum_out=row[:, 2, 1, n:n + 1]).then_inc(probs, 1)
                    if v is not None:
                        hi_half(v + n)

            def peer(layer):
                table_of(ACT.Gelu)
                u0, n = SEG[f"q{layer}"]
                for k in range(n):
                    hi_until(u0 + k + 2)
                    act.wait_ge(half_used, 2 * (u0 + k + 1))
                    bank = sco[k % 2] if k else acc[0]
                    act.activation(qry_t[:, k, :], bank[:, 0:SEQ], ACT.Copy).then_inc(a_read, 1)
                u0, n = SEG[f"u{layer}"]
                for half in range(2):
                    if half:
                        act.wait_ge(listed, layer + 1)
                    else:
                        act.wait_ge(s_rd, (layer + 1) * (LISTS // 4))
                    at = half * (n // 2)
                    with act.Fori(0, n // 2 // RING) as i:
                        for k in range(RING):
                            hi(u0 + at + k + 1, i * RING)
                            act.wait_ge(half_used, i * (2 * RING) + 2 * (u0 + at + k + 1))
                            act.activation(a_t[:, i * RING + (at + k), :], sco[k % 2][:, 0:SEQ],
                                           ACT.Gelu).then_inc(a_read, 1)
                nxt[0] += n
                table_of(ACT.Exp)
                act.wait_ge(shifted, layer + 1)
                act.activation(tops[:], tops[:], ACT.Exp).then_inc(expd, 1)
                act.wait_ge(pk_rd, 3 * (layer + 1))
                with act.Fori(0, SEQ // 4 // HOTS) as i:
                    for k in range(HOTS):
                        act.wait_ge(hot_ready, i * HOTS + (layer * (SEQ // 4) + k + 1))
                        for m in range(4):
                            ins = act.activation(hot1[:, k, m, :], hot1[:, k, m, :], ACT.Copy,
                                                 scale=pick_t[:, 2, bass.ds(i * (4 * HOTS) + (4 * k + m), 1)])
                        ins.then_inc(hot_gated, 1)
                u0, n = SEG[f"v{layer}"]
                act.wait_ge(g_rd, (layer + 1) * (SEQ // 4))
                with act.Fori(0, n // RING - 1) as i:
                    for k in range(RING):
                        gate_tile(layer, i * RING, k)
                        hi(u0 + k + 1, i * RING)
                nxt[0] += n - RING
                for k in range(n - RING, n):
                    gate_tile(layer, 0, k)
                    hi_until(u0 + k + 2)

            def gate_tile(layer, i, k):
                act.wait_ge(half_used, i * 2 + 2 * (SEG[f"v{layer}"][0] + k - 1))
                act.activation(ga_hi[:, k % 2, :], a_t[:, i + k, :], ACT.Copy).then_inc(ga_hi_ready, 1)

            tiles = range(TT)
            act.wait_ge(s_cst, 32)
            table_of(ACT.Sqrt)
            act.wait_ge(s_x[0], 16)
            squares([(h[:, 0, :], xn0[:, 0, :])], [D])
            hi_until(2)
            turn_project("attn0", 0, KC)
            block_out(KC, [(proj[:, 0, k * HB:(k + 1) * HB], acc[k][:, :]) for k in range(2)])
            with act.Fori(1, IN_FULL) as i:
                for k in range(KC):
                    hi(k + 1, i * KC)
                act.wait_ge(half_used, i * (2 * KC) + 2 * KC)
                for half in range(2):
                    act.activation(proj[:, 0, bass.ds(i * UW + half * HB, HB)], acc[half][:, :], ACT.Copy).then_inc(blk_act, 1)
            nxt[0] += (IN_FULL - 1) * KC
            end = SEG["eo"][0]
            hi_until(end - 2)
            heads_out(0, NH0, lambda k: qk_t[:, k, :])
            table_of(ACT.Exp)
            softmax("moba", MOBA_H, sc0, pr0, row0, MOBA_D ** -0.5, 2 * nxt[0])
            nxt[0] += MOBA_H // 2
            block_out(end, [(proj[:, 0, IN_FULL * UW:], acc[0][:, :])])
            act.wait_ge(blk_act, IN_BANKS)
            act.wait_ge(blk_dve, IN_BANKS)
            turn("moba")
            for t in tiles:
                act.activation(proj[:, t, COL_RG:], proj[:, t, COL_RG:], ACT.Silu).then_inc(swish, 1)
            table_of(ACT.Sqrt)
            act.wait_ge(cen_ready, 2)
            act.activation(tmp0[:].rearrange("p k n -> p (k n)")[:, 0:TT * RET_V_W],
                           xn0[:].rearrange("p t n -> p (t n)"), ACT.Square).then_inc(var_ready, 1)
            eo = SEG["eo"][0]
            hi_until(eo + 3)
            act.wait_ge(vsum_ready, 1)
            act.activation(gns[:, 2], gns[:, 1], ACT.Sqrt, bias=eps, scale=1.0 / RET_DV).then_inc(var_ready, 1)
            hi_until(eo + 4)
            turn_project("ret", eo + MOBA_W // P, RET_H)
            table_of(ACT.Sqrt)
            squares([(h[:, 0, :], xn0[:, 0, :])], [D])
            turn("ffn0")
            peer(0)
            table_of(ACT.Sqrt)
            squares([(h[:, 0, :], xn1[:, 0, :])], [D])
            turn_project("attn1", SEG["down"][0], KC)
            block_out(SEG["uq"][0], [(down[:, 0, k * (MLA_DOWN // 2):(k + 1) * (MLA_DOWN // 2)],
                                      acc[k][:, 0:MLA_DOWN // 2]) for k in range(2)])
            squares([(down[:, 0, a:a + n], xn1[:, 0, a:a + n]) for a, n in LATENTS], [Q_RANK, KV_RANK])
            u = SEG["uq"][0]
            turn_project("down", u, Q_RANK // P)
            block_out(u + 4, [(q1[:, 0, k * HB:(k + 1) * HB], acc[k][:, :]) for k in range(2)])
            hi_until(u + 7)
            block_out(u + 6, [(q1[:, 0, UW:], acc[0][:, :])])
            for b in range(2):
                end = SEG["ukv"][0] + 2 * b + 2
                hi_until(end + 1)
                act.wait_ge(half_used, 2 * end)
                for k in range(2):
                    keys_values_out(lambda d, f: act.activation(d, f, ACT.Copy), 0, b, k).then_inc(blk_act, 1)
            table_of(ACT.Exp)
            heads_out(NH0, 2 * MLA_H, lambda k: q_t[:, k, :] if k < MLA_H else k_t[:, k - MLA_H, :])
            softmax("mla", MLA_H, sc1, pr1, row1, MLA_QD ** -0.5)
            table_of(ACT.Sqrt)
            turn_project("heads", SEG["oo"][0], KC)
            squares([(h[:, 0, :], xn1[:, 0, :])], [D])
            turn("ffn1")
            peer(1)
            table_of(ACT.Sqrt)
            squares([(h[:, 0, :], fin[:, 0, :])], [D])

        @block.gpsimd
        def _(pool):
            pool.wait_ge(s_dec, 32)
            for t in range(TT):
                pool.wait_ge(swish, t + 1)
                pool.tensor_tensor(proj[:, t, COL_RG:], proj[:, t, COL_RG:], gnb[:], ALU.mult).then_inc(swish_gain, 1)

        @block.vector
        def _(dve):
            nxt = [0]
            own = [0]

            def tick(ins):
                ins.then_inc(dve_step, 1)
                own[0] += 1

            def settle(at=0):
                dve.wait_ge(dve_step, own[0] + at)

            def then(ins, at=0):
                tick(ins)
                settle(at)

            def lo_half(v, at=0):
                dve.wait_ge(hi_ready, v + 1 + at * 2)
                dve.tensor_tensor(w_lo[:, v % SPLITS, :], raw[:, v // 2 % RING, v % 2 * HB:(v % 2 + 1) * HB],
                                  w_hi[:, v % SPLITS, :].bitcast(F32), ALU.subtract).then_inc(lo_ready, 1)

            def lo(u, at=0):
                lo_half(2 * u, at)
                lo_half(2 * u + 1, at)

            def lo_until(u):
                while nxt[0] < min(u, N_UNITS):
                    lo(nxt[0])
                    nxt[0] += 1

            def chunk(name, c):
                at, c0, _, g = TURN_AT[name]
                dve.wait_ge(turn_hi, at + c + 1)
                hi_t, lo_t = xt(c0 + c)
                src = banks[c % 4][:, 0:SEQ]
                if g is None:
                    ins = dve.tensor_tensor(lo_t, src, hi_t.bitcast(F32), ALU.subtract)
                else:
                    ins = dve.scalar_tensor_tensor(lo_t, src, gain[:, g + c:g + c + 1], hi_t.bitcast(F32),
                                                   ALU.mult, ALU.subtract)
                ins.then_inc(turn_lo, 1)

            def turn(name):
                for c in range(TURN_AT[name][2]):
                    chunk(name, c)

            def turn_project(name, u, n):
                chunk(name, 0)
                chunk(name, 1)
                lo_until(u + 2)
                for k in range(n):
                    if k + 2 < TURN_AT[name][2]:
                        chunk(name, k + 2)
                    lo_until(min(u + k + 3, u + n + 1))

            norms = [0]

            def normed(rows):
                norms[0] += 1
                dve.wait_ge(sq_ready, norms[0])
                then(dve.reciprocal(stat[:, 0:len(rows)], stat[:, 4:4 + len(rows)]))
                for k, (dst, src) in enumerate(rows):
                    ins = dve.tensor_scalar(dst, src, stat[:, k:k + 1], None, ALU.mult)
                ins.then_inc(src_ready, 1)

            def block_out(n, dests):
                dve.wait_ge(half_used, 2 * n)
                for dst, src in dests:
                    dve.tensor_copy(dst, src).then_inc(blk_dve, 1)

            def squares(srcs):
                for k, (src, scratch) in enumerate(srcs):
                    ins = dve.tensor_tensor_reduce(scratch, src, src, 1.0, 0.0, ALU.mult, ALU.add,
                                                   stat[:, TT * k + 1:TT * k + 2])
                ins.then_inc(ms_ready, 1)

            def residual(n, scratch):
                for half in range(2):
                    dve.wait_ge(half_used, 2 * n - 1 + half)
                    for t in range(TT):
                        hs = h[:, t, half * HB:(half + 1) * HB]
                        ins = dve.tensor_tensor(hs, acc[2 * t + half][:, :], hs, ALU.add)
                        if half and t == 0:
                            ins.then_inc(ms_ready, 1)
                then(ins)
                squares([(h[:, 1, :], scratch[:, 1, :])])

            def rope(xv, heads, r2, tab, tmp, tiles):
                a, n = tiles[0], len(tiles)
                cos, sin = table(tab, r2)
                sh = [P, n, heads, r2]
                cb, sb_ = spread(cos[:, a:a + n], sh, 2), spread(sin[:, a:a + n], sh, 2)
                x1, x2 = xv[:, a:a + n, :, 0:r2], xv[:, a:a + n, :, r2:2 * r2]
                t = [tmp[:, k, 0:n * heads * r2].rearrange("p (t h r) -> p t h r", t=n, h=heads) for k in range(4)]
                dve.tensor_tensor(t[0], x1, cb, ALU.mult)
                dve.tensor_tensor(t[1], x2, sb_, ALU.mult)
                dve.tensor_tensor(t[2], x2, cb, ALU.mult)
                then(dve.tensor_tensor(t[3], x1, sb_, ALU.mult))
                dve.tensor_tensor(x1, t[0], t[1], ALU.subtract)
                then(dve.tensor_tensor(x2, t[2], t[3], ALU.add))

            def heads_out(at, n, dst):
                for k in range(1, n, 2):
                    dve.wait_ge(hd_ps, at + k + 1)
                    dve.tensor_copy(dst(k), banks[k % 4][0:dst(k).shape[0], 0:SEQ]).then_inc(hd_dve, 1)

            def outputs(name, b, row, dst, bank=0):
                dve.wait_ge(pv_done, QK_AT[name] + 8 * (b + 1))
                dve.wait_ge(probs, PR_AT[name] + 8 * (b + 1))
                for t in range(TT):
                    ins = dve.reciprocal(row[:, 3, t, 8 * b:8 * b + 8], row[:, 2, t, 8 * b:8 * b + 8])
                then(ins)
                for t in range(TT):
                    ins = dve.tensor_tensor(dst[:, t, b * HB:(b + 1) * HB].rearrange("p (h d) -> p h d", h=8),
                                            acc[2 * t + b + bank][:, :].rearrange("p (h d) -> p h d", h=8),
                                            spread(row[:, 3, t, 8 * b:8 * b + 8], [P, 8, 64], 2), ALU.mult)
                ins.then_inc(src_ready, 1)

            def attend(name, heads, sc, pt, row, scale, dst, v=None):
                at, pa = QK_AT[name], PR_AT[name]
                mask = cst[:, C_MASK:C_MASK + 3 * P]
                for s in range(heads + 1):
                    if s < heads:
                        dve.wait_ge(qk_ps, at + s + 1)
                        if pa + s >= 2:
                            dve.wait_ge(probs, pa + s - 1)
                        for t, (a, b) in enumerate(((0, P), (P, 3 * P))):
                            ins = dve.tensor_tensor_reduce(sc[:, s % 2, a:b], sco[s % 2][:, a:b], mask[:, a:b], 1.0, -3.0e38,
                                                           ALU.add, ALU.max, row[:, 0, t, s:s + 1])
                        then(ins)
                        dve.tensor_scalar(row[:, 1, :, s], row[:, 0, :, s], -scale, None, ALU.mult).then_inc(masked, 1)
                    if s:
                        n = s - 1
                        dve.wait_ge(pt_ps, pa + n + 1)
                        if pa + n >= 2:
                            dve.wait_ge(pv_done, at + n - 1)
                        dve.tensor_copy(pt[:, n % 2, :], trn[n % 2][:, 0:3 * P]).then_inc(pt_ready, 1)
                    if v is not None and s < heads:
                        lo_half(v + s)
                    if s == 10:
                        outputs(name, 0, row, dst)

            def peer(layer):
                u0, n = SEG[f"q{layer}"]
                lo_until(u0 + n + 1)
                for g in range(LISTS // 4):
                    dve.wait_ge(s_ps, layer * (LISTS // 4) + g + 1)
                    k = g // 2 * 8 + g % 2
                    dve.tensor_copy(scores[:, k:k + 7:2, :],
                                    trn[g % 2][:, :].rearrange("p (a n) -> p a n", a=4)).then_inc(s_rd, 1)
                dve.wait_ge(s_rd, (layer + 1) * (LISTS // 4))
                u0, n = SEG[f"u{layer}"]
                GROUPS = 2 * RING
                with dve.Fori(0, n // 2 // RING) as i:
                    for g in range(GROUPS):
                        dve.wait_ge(dve_step, i * GROUPS + (own[0] + g))
                        lo_half(2 * (u0 + 1) + g, i * RING)
                        both = [(lst[:, j, :], v16[:, j, :], n16[:, j, :]) for j in range(2)]
                        if g == 0:
                            ins = dve.tensor_copy(lst[:], scores[:, bass.ds(i * 2, 2), :])
                        elif g == 1:
                            for values, top, _ in both:
                                ins = dve.max(top[:, 0:8], values)
                        elif g == 2:
                            for values, top, at in both:
                                dve.max_index(at[:, 0:8], top[:, 0:8], values)
                                ins = dve.match_replace(values, top[:, 0:8], values, LOWEST)
                        elif g == 3:
                            for values, top, _ in both:
                                ins = dve.max(top[:, 8:16], values)
                        elif g == 4:
                            for values, top, at in both:
                                ins = dve.max_index(at[:, 8:16], top[:, 8:16], values)
                        elif g == 5:
                            dve.tensor_copy(best[:, bass.ds(i * 2, 2), :], v16[:])
                            ins = dve.tensor_copy(best_i[:, bass.ds(i * 2, 2), :], n16[:])
                        else:
                            ins = dve.memset(junk[:, g - 6:g - 5], 0.0)
                        ins.then_inc(dve_step, 1)
                own[0] += GROUPS * (n // 2 // RING)
                dve.wait_ge(dve_step, own[0])
                dve.drain().then_inc(listed, 1)
                sh = [P, TOPK, TOPK]
                sums = cand[:].rearrange("p a b -> p (a b)")
                top, at = v16[:, 0, :], n16[:, 0, :]
                STEPS = GROUPS + 1
                with dve.Fori(0, n // 2 // RING) as i:
                    step = 0
                    for g in range(GROUPS):
                        lo_half(2 * (u0 + n // 2 + 1) + g, i * RING)
                        dve.wait_ge(dve_step, i * STEPS + (own[0] + step))
                        if 1 <= g <= 4:
                            dve.tensor_copy(junk[:, g - 1:g], eps)
                        if g == 0:
                            ins = dve.tensor_tensor(cand[:], spread(best[:, i * 2, :], sh, 2),
                                                    spread(best[:, i * 2 + 1, :], sh, 1), ALU.add)
                        elif g == 1:
                            ins = dve.max(top[:, 0:8], sums)
                        elif g == 2:
                            dve.max_index(at[:, 0:8], top[:, 0:8], sums)
                            ins = dve.match_replace(sums, top[:, 0:8], sums, LOWEST)
                        elif g == 3:
                            ins = dve.max(top[:, 8:16], sums)
                        elif g == 4:
                            ins = dve.max_index(at[:, 8:16], top[:, 8:16], sums)
                        elif g == 5:
                            dve.tensor_copy(tops[:, i, :], top)
                            dve.tensor_scalar(nab[:, 0, :], at, 4, None, ALU.logical_shift_right)
                            ins = dve.tensor_scalar(nab[:, 1, :], at, 15, None, ALU.bitwise_and)
                        elif g == 6:
                            ins = dve.tensor_tensor(eqs[:], spread(nab[:], [P, 2] + sh[1:], 3),
                                                    iota16.unsqueeze(1).unsqueeze(1).to_broadcast([P, 2] + sh[1:]),
                                                    ALU.is_equal)
                        else:
                            ins = dve.tensor_tensor(eqs[:], eqs[:], spread(best_i[:, bass.ds(i * 2, 2), :], [P, 2] + sh[1:], 2),
                                                    ALU.mult)
                            ins.then_inc(dve_step, 1)
                            step += 1
                            dve.wait_ge(dve_step, i * STEPS + (own[0] + step))
                            ins = dve.tensor_reduce(picks[:, 0:2, i, :], eqs[:], AX_X, ALU.add)
                        ins.then_inc(dve_step, 1)
                        step += 1
                assert step == STEPS
                own[0] += STEPS * (n // 2 // RING)
                dve.wait_ge(dve_step, own[0])
                nxt[0] += n
                def hots(i, k):
                    sh4 = [P, 4, P]
                    for q, hot in ((1, hot2), (0, hot1)):
                        ins = dve.tensor_tensor(hot[:, k], spread(iota, sh4, 1), spread(pick_t[:, q, bass.ds(i, 4)], sh4, 2),
                                                ALU.is_equal)
                    ins.then_inc(hot_ready, 1)

                def pick_out(q):
                    dve.wait_ge(pk_ps, 3 * layer + q + 1)
                    dve.tensor_copy(pick_t[:, q, :], trn[q % 2][:, 0:SEQ]).then_inc(pk_rd, 1)

                then(dve.tensor_copy(gsum[:, 0, :], tops[:, :, 0]))
                dve.tensor_tensor(tops[:], tops[:], spread(gsum[:, 0, :], [P, HEADS, TOPK], 2),
                                  ALU.subtract).then_inc(shifted, 1)
                for q in range(2):
                    pick_out(q)
                dve.wait_ge(expd, layer + 1)
                then(dve.tensor_reduce(gsum[:, 0, :], tops[:], AX_X, ALU.add))
                then(dve.reciprocal(gsum[:, 1, :], gsum[:, 0, :]))
                dve.tensor_tensor(picks[:, 2], tops[:], spread(gsum[:, 1, :], [P, HEADS, TOPK], 2),
                                  ALU.mult).then_inc(gated, 1)
                dve.wait_ge(pk_rd, 3 * layer + 2)
                dve.wait_ge(gated, layer + 1)
                hots(0, 0)
                pick_out(2)
                g0 = layer * (SEQ // 4)

                def into_a(i, k):
                    at = a_t[:, :, bass.ds(i, 4)].rearrange("p n t -> p t n")
                    dve.tensor_tensor(at, banks[k][:, :].rearrange("p (t n) -> p t n", t=4), at, ALU.mult).then_inc(g_rd, 1)

                for k in range(1, HOTS):
                    hots(4 * k, k)
                with dve.Fori(0, SEQ // 4 // HOTS - 1) as i:
                    for k in range(HOTS):
                        dve.wait_ge(g_ps, i * HOTS + (g0 + k + 1))
                        into_a(i * (4 * HOTS) + 4 * k, k)
                        hots(i * (4 * HOTS) + 4 * (HOTS + k), k)
                for k in range(HOTS):
                    dve.wait_ge(g_ps, g0 + SEQ // 4 - HOTS + k + 1)
                    into_a(SEQ - 4 * (HOTS - k), k)
                u0, n = SEG[f"v{layer}"]
                dve.wait_ge(g_rd, (layer + 1) * (SEQ // 4))

                def rest(i, k):
                    dve.wait_ge(ga_hi_ready, i + (layer * NKEYS + k + 1))
                    dve.tensor_tensor(ga_lo[:, k % 2, :], a_t[:, i + k, :], ga_hi[:, k % 2, :].bitcast(F32),
                                      ALU.subtract).then_inc(ga_lo_ready, 1)

                with dve.Fori(0, n // RING - 1) as i:
                    for k in range(RING):
                        rest(i * RING, k)
                        lo(u0 + k + 1, i * RING)
                nxt[0] += n - RING
                for k in range(n - RING, n):
                    rest(0, k)
                    lo_until(u0 + k + 2)
                residual(u0 + n, (xn1, fin)[layer])

            tiles = range(TT)
            dve.wait_ge(s_cst, 32)
            dve.tensor_copy(spare[:, 13:14], eps).then_inc(ms_ready, 1)
            for t in tiles:
                dve.wait_ge(s_x[t], 16)
            squares([(h[:, 1, :], xn0[:, 1, :])])
            normed([(xn0[:, t, :], h[:, t, :]) for t in tiles])
            lo_until(2)
            turn_project("attn0", 0, KC)
            block_out(KC, [(proj[:, 1, k * HB:(k + 1) * HB], acc[2 + k][:, :]) for k in range(2)])

            with dve.Fori(1, IN_FULL - 1) as i:
                for k in range(KC):
                    lo(k + 1, i * KC)
                dve.wait_ge(half_used, i * (2 * KC) + 2 * KC)
                for half in range(2):
                    dve.tensor_copy(proj[:, 1, bass.ds(i * UW + half * HB, HB)], acc[2 + half][:, :]).then_inc(blk_dve, 1)
            nxt[0] += (IN_FULL - 2) * KC
            first = (IN_FULL - 1) * KC
            moba_qk = proj[:, :, 0:COL_MV].rearrange("p t (h d) -> p t h d", d=MOBA_D)
            ret_q, ret_k = [proj[:, :, a:a + RET_QK_W].rearrange("p t (h d) -> p t h d", d=RET_DK)
                            for a in (COL_RQ, COL_RQ + RET_QK_W)]
            assert COL_RV <= (IN_FULL - 1) * UW
            lo_until(first + 2)
            dve.wait_ge(s_tab, 16)
            dve.wait_ge(blk_act, 2 * (IN_FULL - 1))
            dve.wait_ge(blk_dve, 2 * (IN_FULL - 1))
            rope(moba_qk, 2 * MOBA_H, MOBA_ROT // 2, C_MROPE, tmp0[:], tiles)
            for k, (view, t) in enumerate(((ret_q, 0), (ret_q, 1), (ret_k, 0), (ret_k, 1))):
                lo_until(first + 3 + k)
                rope(view, RET_H, RET_DK // 2, C_RROPE, tmp0[:], [t])
            dve.tensor_copy(spare[:, 15:16], eps).then_inc(roped, 1)
            end = SEG["eo"][0]
            lo_until(first + KC + 1)
            block_out(first + KC, [(proj[:, 1, (IN_FULL - 1) * UW + k * HB:(IN_FULL - 1) * UW + (k + 1) * HB],
                                    acc[2 + k][:, :]) for k in range(2)])
            lo_until(end - 2)
            heads_out(0, NH0, lambda k: qk_t[:, k, :])
            attend("moba", MOBA_H, sc0, pt0, row0, MOBA_D ** -0.5, cat, 2 * nxt[0])
            nxt[0] += MOBA_H // 2
            block_out(end, [(proj[:, 1, IN_FULL * UW:], acc[2][:, :])])
            outputs("moba", 0, row0, cat, 1)
            turn("moba")
            dve.wait_ge(s_dec, 32)

            def centre(half):
                dve.wait_ge(pv_done, QK_AT["ret"] + 4 * (half + 1))
                means = gns[:, 0, :, 4 * half:4 * half + 4]
                for t in tiles:
                    ins = dve.tensor_reduce(means[:, t], acc[2 * t + half][:, :].rearrange("p (h d) -> p h d", h=4), AX_X, ALU.add)
                then(ins)
                then(dve.tensor_scalar(means, means, 1.0 / RET_DV, None, ALU.mult))
                for t in tiles:
                    ins = dve.tensor_tensor(xn0[:, t, HB * half:HB * (half + 1)].rearrange("p (h d) -> p h d", h=4),
                                            acc[2 * t + half][:, :].rearrange("p (h d) -> p h d", h=4),
                                            spread(means[:, t], [P, 4, RET_DV], 2), ALU.subtract)
                ins.then_inc(cen_ready, 1)

            for n in range(RET_H):
                dve.wait_ge(qk_ps, QK_AT["ret"] + n + 1)
                if n >= 2:
                    dve.wait_ge(pv_done, QK_AT["ret"] + n - 1)
                dve.tensor_tensor(sc0[:, n % 2, 0:SEQ], sco[n % 2][:, 0:SEQ], dec[:, n, :], ALU.mult)
                dve.tensor_tensor(sc0[:, n % 2, SEQ:SEQ + P], sco[n % 2][:, SEQ:SEQ + P], dec[:, n, 0:P],
                                  ALU.mult).then_inc(masked, 1)
                if n == 5:
                    centre(0)
            centre(1)
            dve.wait_ge(var_ready, 1)
            dve.tensor_reduce(gns[:, 1], tmp0[:].rearrange("p k n -> p (k n)")[:, 0:TT * RET_V_W].rearrange(
                "p (t h d) -> p t h d", t=TT, h=RET_H), AX_X, ALU.add).then_inc(vsum_ready, 1)
            eo = SEG["eo"][0]
            lo_until(eo + 3)
            dve.wait_ge(var_ready, 2)
            then(dve.reciprocal(gns[:, 3], gns[:, 2]))
            dve.wait_ge(swish_gain, TT)
            for t in tiles:
                for n in range(RET_H):
                    cols = slice(n * RET_DV, (n + 1) * RET_DV)
                    ins = dve.scalar_tensor_tensor(cat[:, t, MOBA_W + n * RET_DV:MOBA_W + (n + 1) * RET_DV],
                                                   xn0[:, t, cols], gns[:, 3, t, n:n + 1],
                                                   proj[:, t, COL_RG + n * RET_DV:COL_RG + (n + 1) * RET_DV],
                                                   ALU.mult, ALU.mult)
                if t == 0:
                    lo_until(eo + 4)
            ins.then_inc(src_ready, 1)
            turn_project("ret", eo + MOBA_W // P, RET_H)
            residual(SEG["q0"][0], xn0)
            normed([(xn0[:, t, :], h[:, t, :]) for t in tiles])
            turn("ffn0")
            peer(0)

            normed([(xn1[:, t, :], h[:, t, :]) for t in tiles])
            turn_project("attn1", SEG["down"][0], KC)
            block_out(SEG["uq"][0], [(down[:, 1, k * (MLA_DOWN // 2):(k + 1) * (MLA_DOWN // 2)],
                                      acc[2 + k][:, 0:MLA_DOWN // 2]) for k in range(2)])
            dve.wait_ge(blk_act, DOWN_BANKS)
            dve.wait_ge(blk_dve, DOWN_BANKS)
            dve.tensor_copy(spare[:, 14:15], eps).then_inc(ms_ready, 1)
            squares([(down[:, 1, a:a + n], xn1[:, 1, a:a + n]) for a, n in LATENTS])
            normed([(xn1[:, t, a:a + n], down[:, t, a:a + n]) for a, n in LATENTS for t in tiles])
            u = SEG["uq"][0]
            turn_project("down", u, Q_RANK // P)
            block_out(u + 4, [(q1[:, 1, k * HB:(k + 1) * HB], acc[2 + k][:, :]) for k in range(2)])
            lo_until(u + 6)
            rope(down[:, :, Q_RANK + KV_RANK:].rearrange("p t (h d) -> p t h d", h=1), 1, MLA_ROPE // 2, C_LROPE, tmp1[:], tiles)
            for t in tiles:
                tick(dve.tensor_copy(kf[:, t, :].rearrange("p (h d) -> p h d", h=MLA_H)[:, :, MLA_NOPE:],
                                     spread(down[:, t, Q_RANK + KV_RANK:], [P, MLA_H, MLA_ROPE], 1)))
            block_out(u + 6, [(q1[:, 1, UW:], acc[2][:, :])])
            view = q1[:].rearrange("p t (h d) -> p t h d", h=MLA_H)[:, :, :, MLA_NOPE:]
            lo_until(u + 8)
            dve.wait_ge(blk_act, UQ_BANKS)
            dve.wait_ge(blk_dve, UQ_BANKS)
            for b in range(2):
                end = SEG["ukv"][0] + 2 * b + 2
                rope(view, MLA_H, MLA_ROPE // 2, C_LROPE, tmp1[:], [b])
                lo_until(end + 1)
                dve.wait_ge(half_used, 2 * end)
                for k in range(2):
                    keys_values_out(dve.tensor_copy, 1, b, k).then_inc(blk_dve, 1)
            heads_out(NH0, 2 * MLA_H, lambda k: q_t[:, k, :] if k < MLA_H else k_t[:, k - MLA_H, :])
            attend("mla", MLA_H, sc1, pt1, row1, MLA_QD ** -0.5, o1)
            outputs("mla", 1, row1, o1)
            turn_project("heads", SEG["oo"][0], KC)
            residual(SEG["q1"][0], xn1)
            normed([(xn1[:, t, :], h[:, t, :]) for t in tiles])
            turn("ffn1")
            peer(1)

            dve.wait_ge(sq_ready, norms[0] + 1)
            then(dve.reciprocal(stat[:, 0:TT], stat[:, 4:4 + TT]))
            dve.wait_ge(s_fing, 16)
            for t in tiles:
                dve.scalar_tensor_tensor(fin[:, t, :], h[:, t, :], stat[:, t:t + 1], fing[:], ALU.mult,
                                         ALU.mult).then_inc(src_ready, 1)

        @block.tensor
        def _(pe):
            def split(v, at=0):
                pe.wait_ge(lo_ready, v + 1 + at * 2)
                return w_hi[:, v % SPLITS, :], w_lo[:, v % SPLITS, :]

            def unit(u, parts, halves, start, stop, at=0, free=None, centred=False, only=None):
                work = [(v, c, half) for v, (c, half) in enumerate(
                    [(parts[0][0], 0), (parts[0][0], 1)] if len(parts) == 1 else [(c, 0) for c, _ in parts])]
                for v, c, half in (work if only is None else work[only:only + 1]):
                    if centred:
                        pe.wait_ge(cen_ready, half + 1)
                    if free and (v == 0 or half == 1):
                        pe.wait_ge(blk_act, free[half])
                        pe.wait_ge(blk_dve, free[half])
                    w_h, w_l = split(2 * u + v, at)
                    width = halves[half]
                    xh, xl = xt(c)
                    first, last = start and (v == 0 or half == 1), stop and (v == 1 or len(parts) == 1)
                    for t in range(TT):
                        dst = acc[2 * t + half][:, 0:width]
                        th, tl = xh[:, t * P:(t + 1) * P], xl[:, t * P:(t + 1) * P]
                        pe.matmul(dst, th, w_h[:, 0:width], start=first, stop=False)
                        pe.matmul(dst, tl, w_h[:, 0:width], start=False, stop=False)
                        ins = pe.matmul(dst, th, w_l[:, 0:width], start=False, stop=last)
                    ins.then_inc(half_used, 1)

            def project(units, halves, free):
                for n, (u, parts) in enumerate(units):
                    unit(u, parts, halves, n == 0, n == len(units) - 1, 0, free if n == 0 else None)

            def chunk(name, src, c):
                if c == 0:
                    pe.wait_ge(src_ready, TURN_NO[name] + 1)
                if name == "heads" and c == 4:
                    pe.wait_ge(src_ready, TURN_NO[name] + 2)
                if c >= 4:
                    pe.wait_ge(turn_lo, TURN_AT[name][0] + c - 3)
                for t in range(TT):
                    ins = pe.transpose(banks[c % 4][:, t * P:(t + 1) * P], src(c, t), ident)
                ins.then_inc(turn_ps, 1)

            def keep_warm(n):
                for _ in range(n):
                    pe.matmul(banks[3][:, 0:P], ident, ident, start=True, stop=True)

            def columns(src, first=0):
                return lambda c, t: src[:, t, first + c * P:first + (c + 1) * P]

            def turn(name, src):
                at, _, n, _ = TURN_AT[name]
                for c in range(n):
                    chunk(name, src, c)
                pe.wait_ge(turn_lo, at + n)

            def turn_project(name, src, units, halves, start=True):
                at, _, n, _ = TURN_AT[name]
                for c in range(3):
                    chunk(name, src, c)
                for k, (u, parts) in enumerate(units):
                    if k + 3 < n:
                        chunk(name, src, k + 3)
                    pe.wait_ge(turn_lo, at + k + 1)
                    unit(u, parts, halves, start and k == 0, k == len(units) - 1)
                pe.wait_ge(turn_lo, at + n)

            def turn_heads(at, n, src, width):
                for k in range(n):
                    if k >= 4:
                        pe.wait_ge(hd_dve if k % 2 else hd_act, (at + k) // 2 - 1)
                    for t in range(TT):
                        ins = pe.transpose(banks[k % 4][0:width, t * P:(t + 1) * P], src(k, t), ident)
                    ins.then_inc(hd_ps, 1)
                pe.wait_ge(hd_act, (at + n) // 2)
                pe.wait_ge(hd_dve, (at + n) // 2)

            def attend(name, heads, q, k, v, pr, pt, bank=0, between=None):
                at, pa = QK_AT[name], PR_AT[name]
                for s in range(heads + 2):
                    if s < heads:
                        if at + s >= 2:
                            pe.wait_ge(masked, at + s - 1)
                        pe.matmul(sco[s % 2][:, 0:P], q(s)[:, 0:P], k(s)[:, 0:P], start=True, stop=True)
                        pe.matmul(sco[s % 2][:, P:3 * P], q(s)[:, P:SEQ], k(s), start=True, stop=True).then_inc(qk_ps, 1)
                        if between:
                            between(s)
                    if 1 <= s <= heads:
                        n = s - 1
                        pe.wait_ge(probs, pa + n + 1)
                        if pa + n >= 2:
                            pe.wait_ge(pt_ready, pa + n - 1)
                        for b in range(3):
                            ins = pe.transpose(trn[n % 2][:, b * P:(b + 1) * P], pr[:, n % 2, b * P:(b + 1) * P], ident)
                        ins.then_inc(pt_ps, 1)
                    if s >= 2:
                        n = s - 2
                        pe.wait_ge(pt_ready, pa + n + 1)
                        cols = slice((n % 8) * 64, (n % 8) * 64 + 64)
                        o0, o1_ = acc[bank + n // 8][:, cols], acc[2 + bank + n // 8][:, cols]
                        pe.matmul(o0, pt[:, n % 2, 0:P], v(n, 0), start=True, stop=True)
                        pe.matmul(o1_, pt[:, n % 2, P:2 * P], v(n, 0), start=True, stop=False)
                        pe.matmul(o1_, pt[:, n % 2, 2 * P:], v(n, 1), start=False, stop=True).then_inc(pv_done, 1)

            def turned_unit(u, bank, at=0, name=None, src=None):
                dst = (acc[0] if name else sco[bank])[:, 0:SEQ]
                for c in range(KC):
                    if name and c + 3 < KC:
                        chunk(name, src, c + 3)
                    if name:
                        pe.wait_ge(turn_lo, TURN_AT[name][0] + c + 1)
                    if c % 4 == 0:
                        w_h, w_l = split(2 * u + c // 4, at)
                    wh, wl = w_h[:, c % 4 * P:(c % 4 + 1) * P], w_l[:, c % 4 * P:(c % 4 + 1) * P]
                    xh, xl = xt(c)
                    pe.matmul(dst, wh, xh, start=(c == 0), stop=False)
                    pe.matmul(dst, wl, xh, start=False, stop=False)
                    ins = pe.matmul(dst, wh, xl, start=False, stop=(c == KC - 1))
                    if c % 4 == 3:
                        ins.then_inc(half_used, 1)

            def peer(layer):
                b = layer * (PEER_H + NKEYS)
                u0, n = SEG[f"q{layer}"]
                name, src = f"ffn{layer}", columns((xn0, xn1)[layer])
                keep_warm(18)
                for c in range(3):
                    chunk(name, src, c)
                turned_unit(u0, 0, name=name, src=src)
                for k in range(1, n):
                    if k >= 3:
                        pe.wait_ge(a_read, b + k - 1)
                    turned_unit(u0 + k, k % 2)
                b += n
                pe.wait_ge(s_keys, 16 * (layer + 1))
                pe.wait_ge(a_read, b)
                g0 = layer * (LISTS // 4)
                for g in range(LISTS // 4):
                    if g >= 2:
                        pe.wait_ge(s_rd, g0 + g - 1)
                    for m in range(4):
                        t, hh, half = g // 4, g // 2 % 2 * 4 + m, g % 2
                        rows = slice(64 * half, 64 * half + 64)
                        ins = pe.matmul(trn[g % 2][:, m * P:(m + 1) * P], qry_t[rows, hh, t * P:(t + 1) * P],
                                        kys[rows, hh, :], start=True, stop=True)
                    ins.then_inc(s_ps, 1)
                u0, n = SEG[f"u{layer}"]
                with pe.Fori(0, n // (2 * RING)) as i:
                    for k in range(2 * RING):
                        pe.wait_ge(a_read, i * (2 * RING) + (b + k - 1))
                        turned_unit(u0 + k, k % 2, i * (2 * RING))
                pe.wait_ge(shifted, layer + 1)
                for q in range(3):
                    if q == 2:
                        pe.wait_ge(gated, layer + 1)
                        pe.wait_ge(pk_rd, 3 * layer + 1)
                    for t in range(TT):
                        ins = pe.transpose(trn[q % 2][:, t * P:(t + 1) * P],
                                           picks[:, q, t * PEER_H:(t + 1) * PEER_H, :].rearrange("p h k -> p (h k)"), ident)
                    ins.then_inc(pk_ps, 1)
                g0 = layer * (SEQ // 4)

                def gates(i, k, slot):
                    pe.wait_ge(hot_gated, i + (g0 + k + 1))
                    for m in range(4):
                        ins = pe.matmul(banks[slot][:, m * P:(m + 1) * P], hot2[:, slot, m, :].bitcast(F32), hot1[:, slot, m, :],
                                        start=True, stop=True)
                    ins.then_inc(g_ps, 1)

                pe.wait_ge(pk_rd, 3 * layer + 3)
                for k in range(HOTS):
                    gates(0, k, k)
                with pe.Fori(0, SEQ // 4 // HOTS - 1) as i:
                    for k in range(HOTS):
                        pe.wait_ge(g_rd, i * HOTS + (g0 + k + 1))
                        gates(i * HOTS, HOTS + k, k)
                u0, n = SEG[f"v{layer}"]

                def expert_unit(i, k, start, stop):
                    pe.wait_ge(ga_lo_ready, i + (layer * NKEYS + k + 1))
                    for half in range(2):
                        w_h, w_l = split(2 * (u0 + k) + half, i)
                        for t in range(TT):
                            dst = acc[2 * t + half][:, :]
                            ah, al = ga_hi[:, k % 2, t * P:(t + 1) * P], ga_lo[:, k % 2, t * P:(t + 1) * P]
                            pe.matmul(dst, ah, w_h, start=start, stop=False, skip_group_check=True)
                            pe.matmul(dst, al, w_h, start=False, stop=False, skip_group_check=True)
                            ins = pe.matmul(dst, ah, w_l, start=False, stop=stop, skip_group_check=True)
                        ins.then_inc(half_used, 1)

                for k in range(RING):
                    expert_unit(0, k, k == 0, False)
                with pe.Fori(0, n // RING - 2) as i:
                    for k in range(RING):
                        expert_unit(i * RING, RING + k, False, False)
                for k in range(n - RING, n):
                    expert_unit(0, k, False, k == n - 1)

            pe.wait_ge(s_cst, 32)
            keep_warm(18)
            turn_project("attn0", columns(xn0), [(k, [(k, 0)]) for k in range(KC)], [HB, HB])
            with pe.Fori(1, IN_FULL) as i:
                for k in range(KC):
                    unit(k, [(k, 0)], [HB, HB], k == 0, k == KC - 1, i * KC, (i * 2 - 1, i * 2) if k == 0 else None)
            cols = [0, MOBA_W, COL_RQ, COL_RQ + RET_QK_W]
            pe.wait_ge(roped, 1)
            turn_heads(0, NH0, lambda k, t: proj[:, t, cols[k // 4] + (k % 4) * P:cols[k // 4] + (k % 4 + 1) * P], P)
            (units, halves), = blocks_of("in")

            def half_unit(s):
                unit(units[s // 2][0], units[s // 2][1], halves, s < 2, s // 2 == len(units) - 1,
                     free=[2 * IN_FULL] if s == 0 else None, only=s % 2)

            def pair(base):
                return lambda n: qk_t[64 * (n % 2):64 * (n % 2) + 64, base + n // 2, :]

            attend("moba", MOBA_H, pair(0), pair(4), lambda n, t: proj[:, t, COL_MV + n * 64:COL_MV + (n + 1) * 64], pr0, pt0,
                   1, half_unit)
            turn("moba", columns(cat))
            pe.wait_ge(blk_act, IN_BANKS)
            pe.wait_ge(blk_dve, IN_BANKS)
            at = QK_AT["ret"]
            for s in range(RET_H + 1):
                if s < RET_H:
                    pe.wait_ge(masked, at + s - 1)
                    q, k = pair(8)(s), pair(12)(s)
                    pe.matmul(sco[s % 2][:, 0:SEQ], k[:, 0:P], q, start=True, stop=True)
                    pe.matmul(sco[s % 2][:, SEQ:SEQ + P], k[:, P:SEQ], q[:, P:SEQ], start=True, stop=True).then_inc(qk_ps, 1)
                if s:
                    n = s - 1
                    pe.wait_ge(masked, at + n + 1)
                    c = slice((n % 4) * RET_DV, (n % 4 + 1) * RET_DV)
                    v = [proj[:, t, COL_RV + n * RET_DV:COL_RV + (n + 1) * RET_DV] for t in range(TT)]
                    pe.matmul(acc[n // 4][:, c], sc0[:, n % 2, 0:P], v[0], start=True, stop=True)
                    pe.matmul(acc[2 + n // 4][:, c], sc0[:, n % 2, P:SEQ], v[0], start=True, stop=False)
                    pe.matmul(acc[2 + n // 4][:, c], sc0[:, n % 2, SEQ:SEQ + P], v[1], start=False,
                              stop=True).then_inc(pv_done, 1)
            (units, halves), = blocks_of("eo")
            n = MOBA_W // P
            for k, (u, parts) in enumerate(units[:n]):
                unit(u, parts, halves, k == 0, False, centred=(k == 0))
            turn_project("ret", columns(cat, MOBA_W), units[n:], halves, False)
            peer(0)
            (units, halves), = blocks_of("down")
            keep_warm(18)
            turn_project("attn1", columns(xn1), units, halves)
            (units, halves), (units2, halves2) = blocks_of("uq")
            keep_warm(18)
            turn_project("down", columns(xn1), units, halves)
            project(units2, halves2, [DOWN_BANKS + 1])
            for b, (units, halves) in enumerate(blocks_of("ukv")):
                project(units, halves, (UQ_BANKS + b, UQ_BANKS + 2 * b))
            pe.wait_ge(blk_act, UKV_BANKS)
            pe.wait_ge(blk_dve, UKV_BANKS)
            turn_heads(NH0, 2 * MLA_H, lambda k, t: (q1 if k < MLA_H else kf)[:, t, (k % MLA_H) * MLA_QD:(k % MLA_H + 1) * MLA_QD],
                       MLA_QD)
            attend("mla", MLA_H, lambda n: q_t[:, n, :], lambda n: k_t[:, n, :],
                   lambda n, t: v1[:, t, n * MLA_V:(n + 1) * MLA_V], pr1, pt1)
            (units, halves), = blocks_of("oo")
            turn_project("heads", columns(o1), units, halves)
            peer(1)


def kernel(**inputs):
    import numpy as _np
    import concourse.bacc as _bacc
    from concourse import mybir as _mybir
    from concourse.bass_utils import run_bass_kernel_spmd as _run

    a = {k: _np.asarray(v) for k, v in inputs.items()}

    def rows(m):
        return m.reshape(-1, P, UW)

    def halves(m):
        return m.reshape(-1, 2, P, HB).transpose(0, 2, 1, 3).reshape(-1, P, UW)

    def turned(m):
        return m.reshape(-1, P, KC, P).transpose(0, 3, 2, 1).reshape(-1, P, UW)

    def column(v):
        return v.reshape(-1, P).T

    w_in = a["ev_w_in"][0]
    full = IN_FULL * UW
    down = _np.zeros((D, 2, HB), _np.float32)
    down[:, :, :MLA_DOWN // 2] = a["od_w_down"][0].reshape(D, 2, MLA_DOWN // 2)
    uq, ukv = a["od_w_uq"][0], a["od_w_ukv"][0]
    arrays = {
        "w_in": _np.concatenate([rows(w_in[:, k * UW:(k + 1) * UW]) for k in range(IN_FULL)] + [halves(w_in[:, full:])]),
        "w_eo": rows(a["ev_w_o"][0]),
        "w_down": rows(down),
        "w_uq": _np.concatenate([rows(uq[:, :UW]), halves(uq[:, UW:])]),
        "w_ukv": _np.concatenate([rows(ukv[:, :UW]), rows(ukv[:, UW:])]),
        "w_oo": rows(a["od_w_o"][0]),
    }
    for layer in range(2):
        arrays[f"w_q{layer}"] = turned(a["peer_wq"][layer].T)
        arrays[f"w_u{layer}"] = turned(a["peer_u"][layer])
        arrays[f"w_v{layer}"] = rows(a["peer_v"][layer])
    arrays["x"] = a["x"].reshape(TT, P, D).transpose(1, 0, 2)
    arrays["keys"] = a["peer_keys"].transpose(0, 2, 4, 1, 3).reshape(2, P, PEER_H, NKEYS)
    arrays["gains"] = _np.concatenate([column(a["attn_norm"][0]), column(a["ffn_norm"][0]), column(a["attn_norm"][1]),
                                       column(a["ffn_norm"][1]), column(a["od_q_norm"][0]), column(a["od_kv_norm"][0])], axis=1)
    arrays["gn_gain"] = a["ev_ret_gn"][0]
    arrays["fin_gain"] = a["final_norm"]
    arrays["consts"] = constants()
    arrays["decay"] = decay_table()
    arrays = {f"in_{k}_dram": _np.ascontiguousarray(v) for k, v in arrays.items()}

    nc = _bacc.Bacc("TRN2", target_bir_lowering=False, num_devices=1)
    t = {k[3:-5]: nc.dram_tensor(k, v.shape, _mybir.dt.from_np(v.dtype), kind="ExternalInput").ap() for k, v in arrays.items()}
    out = nc.dram_tensor("out_dram", (P, TT, D), _mybir.dt.float32, kind="ExternalOutput").ap()
    build(nc, t["x"], {k[2:]: v for k, v in t.items() if k.startswith("w_")}, t["keys"], t["gains"], t["gn_gain"],
          t["fin_gain"], t["consts"], t["decay"], out)
    r = _run(nc, [arrays], core_ids=[0])
    return r.results[0]["out_dram"].transpose(1, 0, 2).reshape(1, SEQ, D)
```
